# Optimizing a Trainium2 kernel written in Bass

```python
import jax
import jax.numpy as jnp
from jax import lax
import numpy as np
import math
import jax, jax.numpy as jnp

D_MODEL = 1024
BATCH = 1
SEQ = 1024
DEPTH = 1

GRID_W = 64
CTX_LEN = 256
D_MIX = D_MODEL
GLA_WIDTH = D_MIX // 2
GLA_HEADS = 4
GLA_DV = GLA_WIDTH // GLA_HEADS
GLA_DK = GLA_DV // 2
GLA_QK = GLA_HEADS * GLA_DK
GLA_LOWRANK = 16
GLA_TAU = 16.0
GLA_CHUNK = 64
SC_WIDTH = D_MIX - GLA_WIDTH
D_FF = 2816
EPS = 1e-6

COL_K = 0
COL_V = COL_K + GLA_QK
COL_AF = COL_V + GLA_WIDTH
COL_AB = COL_AF + GLA_LOWRANK
COL_Q = COL_AB + GLA_LOWRANK
COL_OG = COL_Q + GLA_QK
COL_SB = COL_OG + GLA_WIDTH
COL_SC = COL_SB + SC_WIDTH
COL_SX = COL_SC + SC_WIDTH
D_IN = COL_SX + SC_WIDTH


def rmsnorm(x, g):
    xf = x.astype(jnp.float32)
    y = xf * lax.rsqrt(jnp.mean(xf * xf, axis=-1, keepdims=True) + EPS)
    return (y * g.astype(jnp.float32)).astype(x.dtype)

def adaln(cond, w, b):
    return jax.nn.silu(cond) @ w + b

def modulate(h, shift, scale):
    return h * (1.0 + scale) + shift

def flip(a):
    return a[:, ::-1]

def gate_logdecay(a_low, w, b):
    a = (a_low @ w + b).astype(jnp.float32)
    return (jax.nn.log_sigmoid(a) / GLA_TAU).reshape(a.shape[0], a.shape[1], GLA_HEADS, GLA_DK)

def gla_inputs(p, w_af, b_af, w_ab, b_ab):
    bsz, t, _ = p.shape
    k = p[..., COL_K:COL_V].reshape(bsz, t, GLA_HEADS, GLA_DK)
    v = p[..., COL_V:COL_AF].reshape(bsz, t, GLA_HEADS, GLA_DV)
    g_f = gate_logdecay(p[..., COL_AF:COL_AB], w_af, b_af)
    g_b = gate_logdecay(p[..., COL_AB:COL_Q], w_ab, b_ab)
    return k, v, g_f, g_b

def gla_final_state(k, v, g):
    b = jnp.cumsum(g.astype(jnp.float32), axis=1)
    w = jnp.exp(b[:, -1:] - b)
    return jnp.einsum('bthk,bthv->bhkv', k.astype(jnp.float32) * w, v.astype(jnp.float32))

def gla_chunked(q, k, v, g, s0, strict):
    bsz, t, h, dk = q.shape
    dv = v.shape[-1]
    n = t // GLA_CHUNK

    def chunks(a):
        a = a.astype(jnp.float32).reshape(bsz, n, GLA_CHUNK, h, a.shape[-1])
        return jnp.moveaxis(a, 1, 0)

    pos = jnp.arange(GLA_CHUNK)
    mask = (pos[None, :] < pos[:, None]) if strict else (pos[None, :] <= pos[:, None])
    mask = mask[None, :, :, None, None]

    def step(s, inp):
        qc, kc, vc, gc = inp
        b = jnp.cumsum(gc, axis=1)
        o_inter = jnp.einsum('bihk,bhkv->bihv', qc * jnp.exp(b), s)
        decay = jnp.exp(jnp.where(mask, b[:, :, None] - b[:, None, :], -jnp.inf))
        att = jnp.einsum('bihk,bjhk,bijhk->bijh', qc, kc, decay)
        o_intra = jnp.einsum('bijh,bjhv->bihv', att, vc)
        b_last = b[:, -1]
        s_new = s * jnp.exp(b_last)[..., None] + jnp.einsum('bjhk,bjhv->bhkv', kc * jnp.exp(b_last[:, None] - b), vc)
        return s_new, o_inter + o_intra

    _, o = lax.scan(step, s0.astype(jnp.float32), (chunks(q), chunks(k), chunks(v), chunks(g)))
    return jnp.moveaxis(o, 0, 1).reshape(bsz, t, h, dv).astype(v.dtype)

def dwconv_row(u, w, b, rows, width):
    bsz, t, ch = u.shape
    up = jnp.pad(u.reshape(bsz, rows, width, ch), ((0, 0), (0, 0), (1, 1), (0, 0)))
    y = w[0] * up[:, :, :-2] + w[1] * up[:, :, 1:-1] + w[2] * up[:, :, 2:] + b
    return y.reshape(bsz, t, ch)

def dwconv_grid(u, w, b, rows, width):
    bsz, t, ch = u.shape
    up = jnp.pad(u.reshape(bsz, rows, width, ch), ((0, 0), (1, 1), (1, 1), (0, 0)))
    y = b
    for dr in range(3):
        for dc in range(3):
            y = y + w[dr, dc] * up[:, dr:dr + rows, dc:dc + width]
    return y.reshape(bsz, t, ch)

def token_mixers(p, s_f, s_b, rows, width, w_af, b_af, w_ab, b_ab, g_head, w_sc, b_sc):
    bsz, t, _ = p.shape
    k, v, g_f, g_b = gla_inputs(p, w_af, b_af, w_ab, b_ab)
    q = p[..., COL_Q:COL_OG].reshape(bsz, t, GLA_HEADS, GLA_DK) * (GLA_DK ** -0.5)
    og = p[..., COL_OG:COL_SB]
    o_f = gla_chunked(q, k, v, g_f, s_f, False)
    o_b = flip(gla_chunked(flip(q), flip(k), flip(v), flip(g_b), s_b, True))
    o_gla = rmsnorm(o_f + o_b, g_head).reshape(bsz, t, GLA_WIDTH) * jax.nn.silu(og)
    sb = p[..., COL_SB:COL_SC]
    sc = p[..., COL_SC:COL_SX]
    sx = p[..., COL_SX:D_IN]
    o_sc = sb * dwconv_row(sc * sx, w_sc, b_sc, rows, width)
    return jnp.concatenate([o_gla, o_sc], axis=-1)

def conv_ffn(h, rows, width, w_up, w_cf, b_cf, w_down):
    u, gate = jnp.split(h @ w_up, 2, axis=-1)
    u = dwconv_grid(u, w_cf, b_cf, rows, width)
    return (jax.nn.silu(u) * gate) @ w_down

def first_inputs(seed: int = 0) -> dict:
    key = jax.random.key(seed)
    ks = jax.random.split(key, 24)

    def nrm(k, shape, s):
        return jax.random.normal(k, shape, jnp.float32) * s

    L = DEPTH
    return {
        'x': nrm(ks[0], (BATCH, SEQ, D_MODEL), 1.0),
        'c': nrm(ks[1], (BATCH, D_MODEL), 1.0),
        'ctx': nrm(ks[2], (BATCH, CTX_LEN, D_MODEL), 1.0),
        'c_ctx': nrm(ks[3], (D_MODEL,), 1.0),
        'w_ada': nrm(ks[4], (L, D_MODEL, 6 * D_MODEL), D_MODEL ** -0.5),
        'b_ada': nrm(ks[5], (L, 6 * D_MODEL), 0.01),
        'g_pre_mix': 1.0 + nrm(ks[6], (L, D_MODEL), 0.05),
        'g_post_mix': 1.0 + nrm(ks[7], (L, D_MODEL), 0.05),
        'g_pre_ffn': 1.0 + nrm(ks[8], (L, D_MODEL), 0.05),
        'g_post_ffn': 1.0 + nrm(ks[9], (L, D_MODEL), 0.05),
        'w_in': nrm(ks[10], (L, D_MODEL, D_IN), D_MODEL ** -0.5),
        'w_af': nrm(ks[11], (L, GLA_LOWRANK, GLA_QK), GLA_LOWRANK ** -0.5),
        'b_af': nrm(ks[12], (L, GLA_QK), 0.1),
        'w_ab': nrm(ks[13], (L, GLA_LOWRANK, GLA_QK), GLA_LOWRANK ** -0.5),
        'b_ab': nrm(ks[14], (L, GLA_QK), 0.1),
        'g_head': 1.0 + nrm(ks[15], (L, GLA_DV), 0.05),
        'w_sc': nrm(ks[16], (L, 3, SC_WIDTH), 0.5),
        'b_sc': nrm(ks[17], (L, SC_WIDTH), 0.01),
        'w_out': nrm(ks[18], (L, D_MIX, D_MODEL), D_MIX ** -0.5),
        'w_up': nrm(ks[19], (L, D_MODEL, 2 * D_FF), D_MODEL ** -0.5),
        'w_cf': nrm(ks[20], (L, 3, 3, D_FF), 1.0 / 3.0),
        'b_cf': nrm(ks[21], (L, D_FF), 0.01),
        'w_down': nrm(ks[22], (L, D_FF, D_MODEL), D_FF ** -0.5),
    }

def first_block(x, c, ctx, c_ctx, w_ada, b_ada, g_pre_mix, g_post_mix, g_pre_ffn, g_post_ffn,
              w_in, w_af, b_af, w_ab, b_ab, g_head, w_sc, b_sc, w_out, w_up, w_cf, b_cf, w_down):
    rows = x.shape[1] // GRID_W
    ctx_len = ctx.shape[1]
    for i in range(DEPTH):
        update_ctx = i + 1 < DEPTH
        sh1, sc1, gt1, sh2, sc2, gt2 = jnp.split(adaln(c, w_ada[i], b_ada[i])[:, None, :], 6, axis=-1)
        csh1, csc1, cgt1, csh2, csc2, cgt2 = jnp.split(adaln(c_ctx, w_ada[i], b_ada[i]), 6, axis=-1)
        gla_p = (w_af[i], b_af[i], w_ab[i], b_ab[i])

        hc = modulate(rmsnorm(ctx, g_pre_mix[i]), csh1, csc1)
        pc = hc @ (w_in[i] if update_ctx else w_in[i][:, :COL_Q])
        kc, vc, gfc, gbc = gla_inputs(pc, *gla_p)
        s_f = gla_final_state(kc, vc, gfc)
        s_b = gla_final_state(flip(kc), flip(vc), flip(gbc))

        hx = modulate(rmsnorm(x, g_pre_mix[i]), sh1, sc1)
        yx = token_mixers(hx @ w_in[i], s_f, s_b, rows, GRID_W, *gla_p, g_head[i], w_sc[i], b_sc[i])
        x = x + gt1 * rmsnorm(yx @ w_out[i], g_post_mix[i])

        hx = modulate(rmsnorm(x, g_pre_ffn[i]), sh2, sc2)
        x = x + gt2 * rmsnorm(conv_ffn(hx, rows, GRID_W, w_up[i], w_cf[i], b_cf[i], w_down[i]), g_post_ffn[i])

        if update_ctx:
            zero_state = jnp.zeros_like(s_f)
            yc = token_mixers(pc, zero_state, zero_state, 1, ctx_len, *gla_p, g_head[i], w_sc[i], b_sc[i])
            ctx = ctx + cgt1 * rmsnorm(yc @ w_out[i], g_post_mix[i])
            hc = modulate(rmsnorm(ctx, g_pre_ffn[i]), csh2, csc2)
            ctx = ctx + cgt2 * rmsnorm(conv_ffn(hc, 1, ctx_len, w_up[i], w_cf[i], b_cf[i], w_down[i]), g_post_ffn[i])
    return x


RWKV_HEAD = 64
RWKV_HEADS = 8
RWKV_DIM = RWKV_HEADS * RWKV_HEAD
W_LORA = 64
A_LORA = 64
G_LORA = 128
DECAY_SCALE = math.exp(-0.5)
LNX_EPS = 64e-5
ATT_HEADS = 8
ATT_KV_HEADS = 2
ATT_HEAD = 64
ATT_DIM = ATT_HEADS * ATT_HEAD
KV_DIM = ATT_KV_HEADS * ATT_HEAD
WINDOW = 128
BLOCK = 128
NEG_INF = -1e30
N_EXPERTS = 16
CAPACITY_FACTOR = 2
EXPERT_FF = 1024
NORM_EPS = 1e-6

RWKV_SPLITS = (RWKV_DIM, 2 * RWKV_DIM, 3 * RWKV_DIM, 3 * RWKV_DIM + G_LORA,
               3 * RWKV_DIM + G_LORA + W_LORA, 3 * RWKV_DIM + G_LORA + 2 * W_LORA,
               3 * RWKV_DIM + G_LORA + 2 * W_LORA + A_LORA)
RWKV_COLS = 3 * RWKV_DIM + G_LORA + 2 * W_LORA + 2 * A_LORA
ATT_SPLITS = (ATT_DIM, ATT_DIM + KV_DIM, ATT_DIM + 2 * KV_DIM, ATT_DIM + 2 * KV_DIM + D_MODEL)
IN_COLS = RWKV_COLS + ATT_DIM + 2 * KV_DIM + 2 * D_MODEL


def rms_norm(x, g):
    xf = x.astype(jnp.float32)
    y = xf * lax.rsqrt(jnp.mean(xf * xf, axis=-1, keepdims=True) + NORM_EPS)
    return (y * g.astype(jnp.float32)).astype(x.dtype)

def centred_token_shift(u, mu_prev, mu_next):
    prev = jnp.pad(u, ((0, 0), (1, 0), (0, 0)))[:, :-1]
    nxt = jnp.pad(u, ((0, 0), (0, 1), (0, 0)))[:, 1:]
    return u + mu_prev * (prev - u) + mu_next * (nxt - u)

def wkv7_scan(r, decay, k, v, kk, a, reverse):
    B, T, H, N = r.shape
    xs = tuple(jnp.moveaxis(t.astype(jnp.float32), 1, 0) for t in (r, decay, k, v, kk, a))

    def step(S, inp):
        r_t, w_t, k_t, v_t, kk_t, a_t = inp
        s_kk = jnp.einsum('bhij,bhj->bhi', S, kk_t)
        S = (S * w_t[:, :, None, :]
             - s_kk[..., None] * (a_t * kk_t)[:, :, None, :]
             + v_t[..., None] * k_t[:, :, None, :])
        return S, jnp.einsum('bhij,bhj->bhi', S, r_t)

    S0 = jnp.zeros((B, H, N, N), jnp.float32)
    _, y = lax.scan(step, S0, xs, reverse=reverse)
    return jnp.moveaxis(y, 0, 1)

def rwkv7_bidir(u, w0_f, w_up_f, w0_b, w_up_b, a0_f, a_up_f, a0_b, a_up_b, g_up, k_k, k_a, r_k, ln_w, ln_b):
    f32 = jnp.float32
    B, T, _ = u.shape
    r, k, v, g_lo, wf_lo, wb_lo, af_lo, ab_lo = jnp.split(u, RWKV_SPLITS, axis=-1)

    def heads(t):
        return t.reshape(B, T, RWKV_HEADS, RWKV_HEAD)

    def decay(w0, lo, up):
        return jnp.exp(-DECAY_SCALE * jax.nn.sigmoid((w0 + jnp.tanh(lo) @ up).astype(f32)))

    def icl_rate(a0, lo, up):
        return jax.nn.sigmoid((a0 + lo @ up).astype(f32))

    kf = k.astype(f32)
    kk = heads(kf * k_k.astype(f32))
    kk = kk / jnp.maximum(jnp.sqrt(jnp.sum(kk * kk, axis=-1, keepdims=True)), 1e-12)
    a_f = icl_rate(a0_f, af_lo, a_up_f)
    a_b = icl_rate(a0_b, ab_lo, a_up_b)
    k_f = heads(kf * (1.0 + (a_f - 1.0) * k_a.astype(f32)))
    k_b = heads(kf * (1.0 + (a_b - 1.0) * k_a.astype(f32)))
    r4 = heads(r.astype(f32))
    v4 = heads(v.astype(f32))

    wkv = (wkv7_scan(r4, heads(decay(w0_f, wf_lo, w_up_f)), k_f, v4, kk, heads(a_f), False)
           + wkv7_scan(r4, heads(decay(w0_b, wb_lo, w_up_b)), k_b, v4, kk, heads(a_b), True))

    mean = jnp.mean(wkv, axis=-1, keepdims=True)
    var = jnp.mean(jnp.square(wkv - mean), axis=-1, keepdims=True)
    normed = ((wkv - mean) * lax.rsqrt(var + LNX_EPS)).reshape(B, T, RWKV_DIM)
    normed = normed * ln_w.astype(f32) + ln_b.astype(f32)

    rk = r_k.astype(f32)
    bonus = ((jnp.sum(r4 * k_f * rk, axis=-1, keepdims=True)
              + jnp.sum(r4 * k_b * rk, axis=-1, keepdims=True)) * v4).reshape(B, T, RWKV_DIM)
    g = (jax.nn.sigmoid(g_lo) @ g_up).astype(f32)
    return ((normed + bonus) * g).astype(u.dtype)

def alibi_slopes(n_heads):
    return 2.0 ** (-8.0 * np.arange(1, n_heads + 1) / n_heads)

def banded_gqa_attention(q, k, v, sink):
    f32 = jnp.float32
    B, T, HQ, DH = q.shape
    G = HQ // ATT_KV_HEADS
    nb = T // BLOCK
    span = BLOCK + 2 * WINDOW
    q = q.reshape(B, T, ATT_KV_HEADS, G, DH) * (DH ** -0.5)
    kp = jnp.pad(k, ((0, 0), (WINDOW, WINDOW), (0, 0), (0, 0)))
    vp = jnp.pad(v, ((0, 0), (WINDOW, WINDOW), (0, 0), (0, 0)))
    slopes = jnp.asarray(alibi_slopes(HQ), f32).reshape(ATT_KV_HEADS, G)
    sink_l = sink.astype(f32).reshape(1, ATT_KV_HEADS, G, 1, 1)
    l_idx = jnp.arange(BLOCK)
    j_idx = jnp.arange(span)
    rel = j_idx[None, :] - WINDOW - l_idx[:, None]
    in_window = jnp.abs(rel) <= WINDOW
    alibi = -slopes[:, :, None, None] * jnp.abs(rel).astype(f32)

    def one_block(i):
        start = i * BLOCK
        qb = lax.dynamic_slice_in_dim(q, start, BLOCK, axis=1)
        kb = lax.dynamic_slice_in_dim(kp, start, span, axis=1)
        vb = lax.dynamic_slice_in_dim(vp, start, span, axis=1)
        key_pos = start - WINDOW + j_idx
        valid = in_window & ((key_pos >= 0) & (key_pos < T))[None, :]
        s = jnp.einsum('blkgd,bjkd->bkglj', qb, kb).astype(f32) + alibi
        s = jnp.where(valid, s, NEG_INF)
        m = jnp.maximum(jnp.max(s, axis=-1, keepdims=True), sink_l)
        p = jnp.exp(s - m)
        denom = jnp.sum(p, axis=-1, keepdims=True) + jnp.exp(sink_l - m)
        return jnp.einsum('bkglj,bjkd->blkgd', (p / denom).astype(vb.dtype), vb)

    out = lax.map(one_block, jnp.arange(nb))
    return jnp.moveaxis(out, 0, 1).reshape(B, T, HQ * DH)

def expert_choice_moe(h, w_router, w_gate, w_up, w_down):
    B, T, D = h.shape
    cap = CAPACITY_FACTOR * T // N_EXPERTS
    affinity = jax.nn.softmax((h @ w_router).astype(jnp.float32), axis=-1)
    top_vals, top_idx = lax.top_k(jnp.swapaxes(affinity, 1, 2), cap)
    b_idx = jnp.arange(B)[:, None, None]
    xs = h[b_idx, top_idx]
    hid = jax.nn.silu(jnp.einsum('becd,edf->becf', xs, w_gate)) * jnp.einsum('becd,edf->becf', xs, w_up)
    ys = jnp.einsum('becf,efd->becd', hid, w_down) * top_vals[..., None].astype(h.dtype)
    return jnp.zeros_like(h).at[b_idx, top_idx].add(ys)

def second_inputs(seed: int = 0) -> dict:
    key = jax.random.key(seed)
    ks = jax.random.split(key, 32)
    L, D, f32 = DEPTH, D_MODEL, jnp.float32
    nrm = lambda k, shape, s: (jax.random.normal(k, shape, f32) * s)
    return {
        'x': nrm(ks[0], (BATCH, SEQ, D), 1.0),
        'norm_mix_g': 1.0 + nrm(ks[1], (L, D), 0.1),
        'w_in': nrm(ks[2], (L, D, IN_COLS), D ** -0.5),
        'mu_prev': jax.random.uniform(ks[3], (L, RWKV_COLS), f32, 0.05, 0.45),
        'mu_next': jax.random.uniform(ks[4], (L, RWKV_COLS), f32, 0.05, 0.45),
        'w0_f': nrm(ks[5], (L, RWKV_DIM), 1.0),
        'w_up_f': nrm(ks[6], (L, W_LORA, RWKV_DIM), 0.5 * W_LORA ** -0.5),
        'w0_b': nrm(ks[7], (L, RWKV_DIM), 1.0),
        'w_up_b': nrm(ks[8], (L, W_LORA, RWKV_DIM), 0.5 * W_LORA ** -0.5),
        'a0_f': nrm(ks[9], (L, RWKV_DIM), 0.5),
        'a_up_f': nrm(ks[10], (L, A_LORA, RWKV_DIM), 0.5 * A_LORA ** -0.5),
        'a0_b': nrm(ks[11], (L, RWKV_DIM), 0.5),
        'a_up_b': nrm(ks[12], (L, A_LORA, RWKV_DIM), 0.5 * A_LORA ** -0.5),
        'g_up': nrm(ks[13], (L, G_LORA, RWKV_DIM), G_LORA ** -0.5),
        'k_k': 0.85 + nrm(ks[14], (L, RWKV_DIM), 0.05),
        'k_a': 1.0 + nrm(ks[15], (L, RWKV_DIM), 0.05),
        'r_k': nrm(ks[16], (L, RWKV_HEADS, RWKV_HEAD), 0.1),
        'ln_x_w': 1.0 + nrm(ks[17], (L, RWKV_DIM), 0.1),
        'ln_x_b': nrm(ks[18], (L, RWKV_DIM), 0.02),
        'attn_sink': nrm(ks[19], (L, ATT_HEADS), 0.5),
        'w_proj_rwkv': nrm(ks[20], (L, RWKV_DIM, D), RWKV_DIM ** -0.5),
        'w_proj_attn': nrm(ks[21], (L, ATT_DIM, D), ATT_DIM ** -0.5),
        'w_out': nrm(ks[22], (L, D, D), D ** -0.5),
        'norm_ffn_g': 1.0 + nrm(ks[23], (L, D), 0.1),
        'w_router': nrm(ks[24], (L, D, N_EXPERTS), D ** -0.5),
        'exp_w_gate': nrm(ks[25], (L, N_EXPERTS, D, EXPERT_FF), D ** -0.5),
        'exp_w_up': nrm(ks[26], (L, N_EXPERTS, D, EXPERT_FF), D ** -0.5),
        'exp_w_down': nrm(ks[27], (L, N_EXPERTS, EXPERT_FF, D), EXPERT_FF ** -0.5),
        'norm_final_g': 1.0 + nrm(ks[28], (D,), 0.1),
    }

def second_block(x, norm_mix_g, w_in, mu_prev, mu_next, w0_f, w_up_f, w0_b, w_up_b, a0_f, a_up_f, a0_b, a_up_b,
              g_up, k_k, k_a, r_k, ln_x_w, ln_x_b, attn_sink, w_proj_rwkv, w_proj_attn, w_out, norm_ffn_g,
              w_router, exp_w_gate, exp_w_up, exp_w_down, norm_final_g):
    B, T, _ = x.shape
    for layer in range(DEPTH):
        h = rms_norm(x, norm_mix_g[layer])
        u = h @ w_in[layer]
        u_rwkv = centred_token_shift(u[..., :RWKV_COLS], mu_prev[layer], mu_next[layer])
        q, k_att, v_att, gl_rwkv, gl_attn = jnp.split(u[..., RWKV_COLS:], ATT_SPLITS, axis=-1)
        y_rwkv = rwkv7_bidir(u_rwkv, w0_f[layer], w_up_f[layer], w0_b[layer], w_up_b[layer],
                             a0_f[layer], a_up_f[layer], a0_b[layer], a_up_b[layer], g_up[layer],
                             k_k[layer], k_a[layer], r_k[layer], ln_x_w[layer], ln_x_b[layer])
        y_attn = banded_gqa_attention(q.reshape(B, T, ATT_HEADS, ATT_HEAD),
                                      k_att.reshape(B, T, ATT_KV_HEADS, ATT_HEAD),
                                      v_att.reshape(B, T, ATT_KV_HEADS, ATT_HEAD), attn_sink[layer])
        merged = (jax.nn.sigmoid(gl_rwkv) * (y_rwkv @ w_proj_rwkv[layer])
                  + jax.nn.sigmoid(gl_attn) * (y_attn @ w_proj_attn[layer]))
        x = x + merged @ w_out[layer]
        x = x + expert_choice_moe(rms_norm(x, norm_ffn_g[layer]), w_router[layer],
                                  exp_w_gate[layer], exp_w_up[layer], exp_w_down[layer])
    return rms_norm(x, norm_final_g)


def setup_inputs(seed=0):
    out = dict(first_inputs(seed))
    for name, value in second_inputs(seed + 1).items():
        if name != "x":
            out[name + "_2"] = value
    return out


def reference(
    x, c, ctx, c_ctx, w_ada, b_ada, g_pre_mix, g_post_mix, g_pre_ffn, g_post_ffn, w_in, w_af,
    b_af, w_ab, b_ab, g_head, w_sc, b_sc, w_out, w_up, w_cf, b_cf, w_down, norm_mix_g_2, w_in_2,
    mu_prev_2, mu_next_2, w0_f_2, w_up_f_2, w0_b_2, w_up_b_2, a0_f_2, a_up_f_2, a0_b_2,
    a_up_b_2, g_up_2, k_k_2, k_a_2, r_k_2, ln_x_w_2, ln_x_b_2, attn_sink_2, w_proj_rwkv_2,
    w_proj_attn_2, w_out_2, norm_ffn_g_2, w_router_2, exp_w_gate_2, exp_w_up_2, exp_w_down_2,
    norm_final_g_2,
):
    x = first_block(
        x, c, ctx, c_ctx, w_ada, b_ada, g_pre_mix, g_post_mix, g_pre_ffn, g_post_ffn, w_in,
        w_af, b_af, w_ab, b_ab, g_head, w_sc, b_sc, w_out, w_up, w_cf, b_cf, w_down,
    )
    return second_block(
        x, norm_mix_g_2, w_in_2, mu_prev_2, mu_next_2, w0_f_2, w_up_f_2, w0_b_2, w_up_b_2,
        a0_f_2, a_up_f_2, a0_b_2, a_up_b_2, g_up_2, k_k_2, k_a_2, r_k_2, ln_x_w_2, ln_x_b_2,
        attn_sink_2, w_proj_rwkv_2, w_proj_attn_2, w_out_2, norm_ffn_g_2, w_router_2,
        exp_w_gate_2, exp_w_up_2, exp_w_down_2, norm_final_g_2,
    )


_drawn_inputs = setup_inputs


def setup_inputs(seed=0):
    import zlib

    import numpy as np

    out = dict(_drawn_inputs(seed))
    spreads = {}
    factors = {'ctx': 2.711,
     'b_af': 3.37,
     'b_ab': 4.019,
     'g_head': 3.253,
     'b_sc': 8.0,
     'b_cf': 8.0,
     'w_up_f_2': 5.1,
     'w_up_b_2': 5.134,
     'k_k_2': 7.899,
     'k_a_2': 3.494,
     'ln_x_b_2': 8.0,
     'attn_sink_2': 8.0}
    for name, (base, spread) in spreads.items():
        noise = np.random.default_rng([zlib.crc32(name.encode()), seed]).standard_normal(out[name].shape)
        drawn = base * np.exp(spread * noise) if base else spread * noise
        out[name] = jnp.asarray(drawn.astype(out[name].dtype))
    for name, factor in factors.items():
        out[name] = (out[name] * factor).astype(out[name].dtype)
    return out
```

```python
from contextlib import ExitStack

import numpy as np
import concourse.bass as bass
import concourse.mybir as mybir

F32 = mybir.dt.float32
F32R = mybir.dt.float32r
U32 = mybir.dt.uint32
ALU = mybir.AluOpType
ACT = mybir.ActivationFunctionType
AX = mybir.AxisListType.X
P = 128
KB = 1024

D = 1024
T = 1024
CT = 256
TT, CTT = T // P, CT // P
KD = D // P
NH, DK, DV = 4, 64, 128
QK, GV = NH * DK, NH * DV
LOWR = 16
TAU = 16.0
CH = 128
SCW = 512
FF = 2816
FB = FF // P
EPS = 1e-6
GRID_W = 64
GRID_H = T // GRID_W
C_K, C_V, C_AF, C_Q = 0, 256, 768, 800
C_OG, C_SB, C_SC, C_SX = 1056, 1568, 2080, 2592
RD, RH, RN = 512, 8, 64
RC = 1920
RB = RC // P
C2_Q, C2_K, C2_V, C2_GR, C2_GA = 1920, 2432, 2560, 2688, 3712
DECAY_SCALE = float(np.exp(-0.5))
LNX_EPS = 64e-5
AH, AKV, ADH, WIN = 8, 2, 64, 128
NE, CAP, EF = 16, 128, 1024
NEG = -1e30

LEVELS = 7
M_ID, M_UI, M_US, M_LI, M_LS, M_BO, M_LO = 0, 1, 2, 3, 4, 5, 6
M_UP = M_LO + LEVELS
N_MASKS = M_UP + LEVELS


def mask_table():
    r, c = np.arange(P)[:, None], np.arange(P)[None, :]
    m = [r == c, r <= c, r < c, r >= c, r > c, r // 64 == c // 64]
    low = [(r >> (l + 1) == c >> (l + 1)) & ((r >> l) % 2 == 1) & ((c >> l) % 2 == 0) for l in range(LEVELS)]
    m += low + [x.T for x in low]
    return np.concatenate([x.astype(np.float32) for x in m], axis=1)


def alibi_table():
    rel = np.arange(3 * P)[None, :] - WIN - np.arange(P)[:, None]
    slopes = 2.0 ** (-8.0 * np.arange(1, AH + 1) / AH)
    t = -slopes[None, :, None].astype(np.float32) * np.abs(rel)[:, None, :].astype(np.float32)
    return np.where(np.abs(rel)[:, None, :] <= WIN, t, np.float32(NEG)).astype(np.float32)


PARAM_ROWS = [
    [("w_cf", 0, 128)],
    [("w_cf", 128, 70), ("b_cf", 0, 22), ("w_sc", 0, 12), ("b_sc", 0, 4), ("b_af", 0, 2), ("b_ab", 0, 2)],
    [("mu_prev_2", 0, 15), ("mu_next_2", 0, 15), ("w0_f_2", 0, 4), ("w0_b_2", 0, 4), ("a0_f_2", 0, 4),
     ("a0_b_2", 0, 4), ("k_k_2", 0, 4), ("k_a_2", 0, 4), ("r_k_2", 0, 4), ("ln_x_w_2", 0, 4),
     ("ln_x_b_2", 0, 4)],
]


def param_columns():
    col = {}
    for t, rows in enumerate(PARAM_ROWS):
        at = 0
        for name, first, n in rows:
            col.setdefault(name, t * P + at - first)
            at += n
    return col


PCOL = param_columns()


class Core:

    BANKS, BANK = 3, 52
    FIRST = 16512

    def __init__(self, nc, dram):
        self.nc, self.dram, self.stages = nc, dram, 0
        self.psum = nc.alloc_psum_tensor("psum", [P, 8, 512], F32)
        self.masks = self.at("masks", 0, [P, N_MASKS, P])
        self.pcol = self.at("param_columns", 10.5, [P, 3 * P])
        self.x = self.at("x_stream", 44, [P, TT, D])

    def at(self, name, kb, shape, dtype=F32):
        return self.nc.alloc_sbuf_tensor_at(name, shape, dtype, offset=Core.FIRST + int(kb * KB))

    def param_source(self, name):
        a = self.dram[name]
        if name == "r_k_2":
            return a.rearrange("l (b h) n -> (l b) (h n)", h=2)
        lead = "abcd"[:len(a.shape) - 1]
        names = " ".join(lead)
        return a.rearrange(f"{names} (n p) -> ({names} n) p", p=P)

    def mask(self, m):
        return self.masks[:, m, :]

    def col(self, name, n=0, rows=P):
        c = PCOL[name] + n
        return self.pcol[0:rows, c:c + 1]


class Stage:

    def __init__(self, core, name):
        self.core, self.nc, self.name = core, core.nc, name

    def __enter__(self):
        n = self.core.stages
        self.core.stages += 1
        self.first = 100 + (n % Core.BANKS) * Core.BANK
        self.handles = []
        self.block = self.nc.Block()
        opened = self.block.__enter__()
        before = 100 + ((n + 2) % Core.BANKS) * Core.BANK
        if n > 0:
            @opened.gpsimd
            def _(pool):
                pool.sem_clear(range(before, before + Core.BANK))
        self.b = opened
        return self

    def sem(self, name):
        assert len(self.handles) < Core.BANK
        h = self.nc.alloc_semaphore(f"{self.name}_{name}", self.first + len(self.handles))
        self.handles.append(h)
        return h

    def sems(self, *names):
        return [self.sem(n) for n in names]

    def __exit__(self, *e):
        r = self.block.__exit__(*e)
        for h in self.handles:
            self.nc.release_semaphore(h)
        return r


def run_loop(eng, n, body):
    body(0, None)
    if n > 1:
        with eng.Fori(0, n - 1) as before:
            body(before + 1, before)


def passed(eng, sem):
    eng.sem_inc(sem, 1)


def high_part(nc, out, src, scale=1.0):
    return nc.scalar.activation(out, src, ACT.Copy, scale=scale)


def low_part(nc, out, src, high):
    return nc.vector.tensor_tensor(out, src, high.bitcast(F32), ALU.subtract)


def split_product(nc, out, left, right, start, stop):
    nc.tensor.matmul(out, left[0], right[0], start=start, stop=False)
    nc.tensor.matmul(out, left[0], right[1], start=False, stop=False)
    return nc.tensor.matmul(out, left[1], right[0], start=False, stop=stop)


R_SH1, R_G1, R_GP1, R_SH2, R_G2, R_GP2, R_CSH, R_CG = range(8)


def stage_modulation(core):
    nc, dram, ps = core.nc, core.dram, core.psum
    rows = core.rows = core.at("mod_rows", 12, [P, 8, D])
    flat_rows = rows.ap().rearrange("p a d -> p (a d)")
    NW = 4
    ada_w = core.at("ada_weights", 44, [P, NW, KD, 512])
    cvec = core.at("cond_vectors", 108, [P, 2, KD])
    csil = core.at("cond_silu", 108.25, [P, 2, KD])
    ones = core.at("ones", 109, [P, P])
    graw = core.at("gain_rows", 150, [P, 4, D])
    praw = core.at("param_rows", 166, [P, 3, P])
    core.ctx = core.at("ctx_tiles", 170, [P, CTT, D])
    core.x0 = core.at("x_tiles", 116, [P, TT, D])
    with Stage(core, "mod") as s:
        (masks_in, x_in, ctx_in, cond_in, param_in, bias_in, gain_in, silu_done, zeroed, params_turned,
         params_out, rows_done, ctx_rows_done, combined, order, sum_mm, ctx_sum, ctx_mm) = s.sems(
            "masks_in", "x_in", "ctx_in", "cond_in", "param_in", "bias_in", "gain_in", "silu_done",
            "zeroed", "params_turned", "params_out", "rows_done", "ctx_rows_done", "combined", "order",
            "sum_mm", "ctx_sum", "ctx_mm")
        w_in = [s.sem(f"w_in{j}") for j in range(NW)]
        summed = [s.sem(f"summed{j}") for j in range(NW)]
        n_par = sum(len(t) for t in PARAM_ROWS)

        @s.b.gpsimd
        def _(pool):
            nc.gpsimd.memset(rows[:], 0.0).then_inc(zeroed, 1)
            nc.gpsimd.memset(ones[:], 1.0).then_inc(zeroed, 1)

        @s.b.sync
        def _(sp):
            with nc.allow_non_contiguous_dma(reason="short vectors"):
                for v, name in enumerate(("c", "c_ctx")):
                    src = dram[name].rearrange("a d -> (a d)") if name == "c" else dram[name]
                    sp.dma_start(cvec[:, v, :], src.rearrange("(p k) -> p k", k=KD)).then_inc(cond_in, 16)

            def load(i, before):
                for j in range(NW):
                    if before is not None:
                        sp.wait_ge(summed[j], i)
                    sp.dma_start(ada_w[:, j], dram["w_ada"][0].rearrange("(p k) n -> p k n", k=KD)
                                 [:, :, bass.ds(i * (512 * NW) + 512 * j, 512)]).then_inc(w_in[j], 16)
            run_loop(sp, 3, load)

        @s.b.scalar
        def _(act):
            act.wait_ge(cond_in, 32)
            nc.scalar.activation(csil[:], cvec[:], ACT.Silu).then_inc(silu_done, 1)
            act.wait_ge(zeroed, 1)
            act.dma_start(flat_rows[0:1, 0:6 * D], dram["b_ada"]).then_inc(bias_in, 16)
            act.dma_start(flat_rows[0:1, 6 * D:8 * D], dram["b_ada"][:, 0:2 * D]).then_inc(bias_in, 16)
            act.dma_start(core.masks.ap().rearrange("p a b -> p (a b)"), dram["masks"]).then_inc(masks_in, 16)
            for t, parts in enumerate(PARAM_ROWS):
                at = 0
                for name, first, n in parts:
                    act.dma_start(praw[at:at + n, t, :], core.param_source(name)[first:first + n, :]).then_inc(
                        param_in, 16)
                    at += n
            act.dma_start(core.ctx[:], dram["ctx"][0].rearrange("(t p) d -> p t d", p=P)).then_inc(ctx_in, 16)
            act.dma_start(core.x0[:], dram["x"][0].rearrange("(t p) d -> p t d", p=P)).then_inc(x_in, 16)
            for g, name in enumerate(("g_pre_mix", "g_post_mix", "g_pre_ffn", "g_post_ffn")):
                act.dma_start(graw[:, g, :], dram[name].to_broadcast([P, D])).then_inc(gain_in, 16)

            def evacuate(i, before):
                for j in range(NW):
                    if before is None:
                        act.wait_ge(ctx_mm, j + 1)
                        nc.scalar.activation(flat_rows[:, 6 * D + 512 * j:6 * D + 512 * j + 512],
                                             ps[:, 4 + (j + 1) % 4, :], ACT.Copy).then_inc(ctx_rows_done, 1)
                    act.wait_ge(sum_mm, i * NW + (j + 1))
                    nc.scalar.activation(flat_rows[:, bass.ds(i * (512 * NW) + 512 * j, 512)], ps[:, j, :], ACT.Copy
                                         ).then_inc(rows_done, 1)
            run_loop(act, 3, evacuate)

        @s.b.vector
        def _(dve):
            dve.wait_ge(silu_done, 1)
            dve.wait_ge(bias_in, 32)

            def sums(i, before):
                for j in range(NW):
                    dve.wait_ge(w_in[j], i * 16 + 16)
                    chains = [(0, flat_rows[:, bass.ds(i * (512 * NW) + 512 * j, 512)], summed[j])]
                    if before is None:
                        chains.insert(0, (1, flat_rows[:, 6 * D + 512 * j:6 * D + 512 * j + 512], ctx_sum))
                    for n, (v, acc, done) in enumerate(chains):
                        at = 7 * (2 * j + n) if before is None else i * (7 * NW) + (7 * NW + 7 * j)
                        for k in range(KD):
                            if k:
                                dve.wait_ge(order, at + k)
                            nc.vector.scalar_tensor_tensor(out=acc, in0=ada_w[:, j, k], scalar=csil[:, v, k:k + 1],
                                                           in1=acc, op0=ALU.mult, op1=ALU.add
                                                           ).then_inc(order if k < KD - 1 else done, 1)
            run_loop(dve, 3, sums)
            dve.wait_ge(params_turned, 1)
            for t, parts in enumerate(PARAM_ROWS):
                n = sum(x[2] for x in parts)
                nc.vector.tensor_copy(core.pcol[:, t * P:t * P + n], ps[:, 7, t * P:t * P + n]).then_inc(params_out, 1)
            dve.wait_ge(gain_in, 64)
            dve.wait_ge(rows_done, 12)
            dve.wait_ge(ctx_rows_done, 4)
            for r, g in ((R_G1, 0), (R_G2, 2), (R_CG, 0)):
                nc.vector.scalar_tensor_tensor(out=rows[:, r], in0=rows[:, r], scalar=1.0, in1=graw[:, g],
                                               op0=ALU.add, op1=ALU.mult).then_inc(combined, 1)
            for r, g in ((R_GP1, 1), (R_GP2, 3)):
                nc.vector.tensor_tensor(rows[:, r], rows[:, r], graw[:, g], ALU.mult).then_inc(combined, 1)
            dve.wait_ge(combined, 5)
            dve.wait_ge(x_in, 16)
            dve.wait_ge(ctx_in, 16)

        @s.b.tensor
        def _(pe):
            pe.wait_ge(zeroed, 2)

            def products(i, before):
                for j in range(NW):
                    if before is None:
                        pe.wait_ge(ctx_sum, j + 1)
                        nc.tensor.matmul(ps[:, 4 + (j + 1) % 4, :], ones[:],
                                         flat_rows[:, 6 * D + 512 * j:6 * D + 512 * j + 512], start=True, stop=True
                                         ).then_inc(ctx_mm, 1)
                    pe.wait_ge(summed[j], i + 1)
                    if before is not None:
                        pe.wait_ge(rows_done, before * NW + (j + 1))
                    nc.tensor.matmul(ps[:, j, :], ones[:], flat_rows[:, bass.ds(i * (512 * NW) + 512 * j, 512)],
                                     start=True, stop=True).then_inc(sum_mm, 1)
            run_loop(pe, 3, products)
            pe.wait_ge(masks_in, 16)
            pe.wait_ge(param_in, 16 * n_par)
            pe.wait_ge(ctx_rows_done, 4)
            for t, parts in enumerate(PARAM_ROWS):
                n = sum(x[2] for x in parts)
                ins = nc.tensor.transpose(ps[:, 7, t * P:t * P + n], praw[0:n, t, :], core.masks[0:n, M_ID, 0:n])
            ins.then_inc(params_turned, 1)


def stage_norm_turn(core, name, jobs, scratch_kb, store=None, load=()):
    nc, ps = core.nc, core.psum
    tiles = [(src[:, t], gain, shift, dst, first + t * P) for src, n, gain, shift, dst, first in jobs
             for t in range(n)]
    nt = len(tiles)
    hbuf = core.at(f"{name}_h", scratch_kb, [P, 2, D])
    junk = core.at(f"{name}_junk", scratch_kb + 8, [P, D])
    stat = core.at(f"{name}_stat", scratch_kb + 12, [P, 3, 16])
    split = isinstance(tiles[0][3], tuple)
    with Stage(core, name) as s:
        rows_in, squares, root_in, rooted, inverse, scaled, normed, turned = s.sems(
            "rows_in", "squares", "root_in", "rooted", "inverse", "scaled", "normed", "turned")
        stored = [s.sem("stored0"), s.sem("stored1")]
        out_done = [s.sem("out0"), s.sem("out1")]

        def banks(t):
            b = 2 * (t % 4)
            return ps[:, b:b + 2, :].rearrange("p b (k t) -> p (b k) t", t=P)

        @s.b.scalar
        def _(act):
            nc.scalar.preload_act_table(ACT.Sqrt)

            def square(t):
                if t:
                    act.wait_ge(squares, t)
                nc.scalar.activation(junk[:], tiles[t][0], ACT.Square, accum_out=stat[:, 0, t:t + 1]
                                     ).then_inc(squares, 1)

            def out(t):
                dst, first = tiles[t][3:]
                act.wait_ge(turned, t + 1)
                if split:
                    high_part(nc, dst[0][:, :, first:first + P], banks(t)).then_inc(out_done[1], 1)
                else:
                    nc.scalar.activation(dst[:, 4:8, first:first + P], banks(t)[:, 4:8], ACT.Copy
                                         ).then_inc(out_done[1], 1)
            square(0)
            square(1)
            for t in range(nt):
                act.wait_ge(root_in, t + 1)
                nc.scalar.activation(stat[:, 2, t:t + 1], stat[:, 1, t:t + 1], ACT.Sqrt).then_inc(rooted, 1)
                if t + 2 < nt:
                    square(t + 2)
                if t:
                    out(t - 1)
            out(nt - 1)

        @s.b.vector
        def _(dve):
            def mean(t):
                dve.wait_ge(squares, t + 1)
                nc.vector.tensor_scalar(stat[:, 1, t:t + 1], stat[:, 0, t:t + 1], 1.0 / D, EPS, ALU.mult, ALU.add
                                        ).then_inc(root_in, 1)

            def out(t):
                dst, first = tiles[t][3:]
                dve.wait_ge(turned, t + 1)
                if split:
                    dve.wait_ge(out_done[1], t + 1)
                    low_part(nc, dst[1][:, :, first:first + P], banks(t), dst[0][:, :, first:first + P]
                             ).then_inc(out_done[0], 1)
                else:
                    nc.vector.tensor_copy(dst[:, 0:4, first:first + P], banks(t)[:, 0:4]).then_inc(out_done[0], 1)
            mean(0)
            if load:
                dve.wait_ge(rows_in, 16 * len(load))
            for t, (src, gain, shift, _, _) in enumerate(tiles):
                dve.wait_ge(rooted, t + 1)
                nc.vector.reciprocal(stat[:, 0, t:t + 1], stat[:, 2, t:t + 1]).then_inc(inverse, 1)
                dve.wait_ge(inverse, t + 1)
                if t >= 2:
                    dve.wait_ge(turned, t - 1)
                    if store is not None:
                        dve.wait_ge(stored[t % 2], 16 * (t // 2))
                nc.vector.scalar_tensor_tensor(out=hbuf[:, t % 2], in0=src, scalar=stat[:, 0, t:t + 1], in1=gain,
                                               op0=ALU.mult, op1=ALU.mult
                                               ).then_inc(normed if shift is None else scaled, 1)
                if t + 1 < nt:
                    mean(t + 1)
                if t:
                    out(t - 1)
            out(nt - 1)

        @s.b.gpsimd
        def _(pool):
            for t, (_, _, shift, _, _) in enumerate(tiles):
                if shift is not None:
                    pool.wait_ge(scaled, t + 1)
                    nc.gpsimd.tensor_tensor(hbuf[:, t % 2], hbuf[:, t % 2], shift, ALU.add).then_inc(normed, 1)

        @s.b.tensor
        def _(pe):
            for t in range(nt):
                pe.wait_ge(normed, t + 1)
                if t >= 4:
                    pe.wait_ge(out_done[0], t - 3)
                    pe.wait_ge(out_done[1], t - 3)
                for k in range(KD):
                    ins = nc.tensor.transpose(ps[:, 2 * (t % 4) + k // 4, (k % 4) * P:(k % 4 + 1) * P],
                                              hbuf[:, t % 2, k * P:(k + 1) * P], core.mask(M_ID))
                ins.then_inc(turned, 1)

        @s.b.sync
        def _(sp):
            for row, src in load:
                sp.dma_start(row, src).then_inc(rows_in, 16)
            if store is not None:
                for t in range(nt):
                    sp.wait_ge(normed, t + 1)
                    sp.dma_start(store[t * P:(t + 1) * P, :], hbuf[:, t % 2]).then_inc(stored[t % 2], 16)
                for j in range(2):
                    sp.wait_ge(stored[j], 16 * (nt // 2))


def weight_columns(w, first, n):
    return w.rearrange("(k p) n -> p k n", p=P)[:, :, bass.ds(first, n)]


def stage_project_mix(core):
    nc, dram, ps = core.nc, core.dram, core.psum
    w_in = dram["w_in"][0]
    NT = CTT + TT
    flat = ps.ap().rearrange("p b n -> p (b n)")
    kT = core.kT = core.at("kT", 116, [P, 2, NT * P])
    qT = core.qT = core.at("qT", 126, [P, 2, T])
    v = core.v = core.at("v_tm", 134, [P, NT, GV])
    og = core.og = core.at("out_gate", 154, [P, TT, GV])
    osc = core.osc = core.at("conv_out", 170, [P, 4, T])
    low = core.low = core.at("gate_low", 186, [2 * LOWR, NT * P])
    wt = core.at("w_tm", 36, [P, 2, GV])
    wt_split = core.at("w_tm_split", 191, [P, 2, 2, GV], F32R)
    wc = core.at("w_cm", 36, [P, KD, P])
    wc_split = core.at("w_cm_split", 191, [P, 2, 2, KD, P], F32R)
    scx = core.at("sc_part", 40, [P, T])

    def tokens(k, t0, n):
        part = core.hT_ctx if t0 < CT else core.hT_x
        t0 -= 0 if t0 < CT else CT
        return [a[:, k, t0:t0 + n] for a in part]

    groups = [(C_V, (0, 1, 2, 3)), (C_V, (4, 5, 6, 7)), (C_V, (8, 9)),
              (C_OG, (2, 3, 4, 5)), (C_OG, (6, 7, 8, 9))]
    kinds = [("low", C_AF), ("k0", C_K), ("k1", C_K + P), ("q0", C_Q), ("q1", C_Q + P)]
    for n in range(4):
        kinds += [("sc", C_SC + P * n), ("sx", C_SX + P * n), ("sb", C_SB + P * n)]
    NQ, NB = len(groups) * KD, len(kinds)
    irregular = 5
    with Stage(core, "mix") as s:
        (tm_in0, tm_in1, tm_high, tm_low, tm_used, tm_mm, v_out, og_out, cm_in, cm_high, cm_low, cm_mm, cm_out,
         sc_out, sx_out, conv_done, order) = s.sems(
            "tm_in0", "tm_in1", "tm_high", "tm_low", "tm_used", "tm_mm", "v_out", "og_out", "cm_in", "cm_high",
            "cm_low", "cm_mm", "cm_out", "sc_out", "sx_out", "conv_done", "order")
        tm_in = (tm_in0, tm_in1)
        first_tile = [sum(len(g[1]) for g in groups[:n]) for n in range(len(groups) + 1)]
        NV = first_tile[3]

        def out_of(eng, n):
            if n > 0:
                eng.wait_ge(*((v_out, n) if n <= NV else (og_out, n - NV)))

        def banks(n):
            return 0 if n < irregular and n % 2 == 0 else 4 if n < irregular else 2 * ((n - irregular) % 3)

        @s.b.sync
        def _(sp):
            for q in range(NQ):
                g, k = divmod(q, KD)
                if q >= 2:
                    sp.wait_ge(tm_low, q - 1)
                sp.dma_start(wt[:, q % 2], w_in[k * P:(k + 1) * P, groups[g][0]:groups[g][0] + GV]
                             ).then_inc(tm_in[q % 2], 16)
            sp.wait_ge(tm_low, NQ)
            for n, (_, first) in enumerate(kinds):
                if n:
                    sp.wait_ge(cm_low, n)
                sp.dma_start(wc[:], weight_columns(w_in, first, P)).then_inc(cm_in, 16)

        @s.b.tensor
        def _(pe):
            for q in range(NQ):
                g, k = divmod(q, KD)
                pe.wait_ge(tm_low, q + 1)
                for a, t in enumerate(groups[g][1]):
                    if k == 0 and g >= 2:
                        out_of(pe, min(first_tile[g - 2] + a + 1, first_tile[g - 1]))
                    ins = split_product(nc, ps[:, 4 * (g % 2) + a, :], tokens(k, t * P, P),
                                        [wt_split[:, q % 2, m] for m in range(2)], k == 0, k == KD - 1)
                    if k == KD - 1:
                        ins.then_inc(tm_mm, 1)
                if k < KD - 1:
                    ins.then_inc(tm_used, 1)
            out_of(pe, NV)
            out_of(pe, NV + TT)
            for n, (kind, _) in enumerate(kinds):
                pe.wait_ge(cm_low, n + 1)
                b = banks(n)
                if n < irregular + 3:
                    if n >= 2:
                        pe.wait_ge(cm_out, min(n - 1, irregular) if n < irregular else irregular)
                else:
                    m = (n - irregular) // 3
                    pe.wait_ge({"sc": sc_out, "sx": sx_out, "sb": conv_done}[kind], m)
                parts = ((0, CT), (CT, 512), (CT + 512, 512)) if n < irregular else ((CT, 512), (CT + 512, 512))
                for a, (t0, tn) in enumerate(parts):
                    if kind[0] == "q" and t0 == 0:
                        continue
                    for k in range(KD):
                        ins = split_product(nc, ps[:, b + a, 512 - tn:512],
                                            [wc_split[:, n % 2, m, k] for m in range(2)], tokens(k, t0, tn),
                                            k == 0, k == KD - 1)
                ins.then_inc(cm_mm, 1)

        @s.b.scalar
        def _(act):
            nc.scalar.preload_act_table(ACT.Silu)

            def gate(n):
                act.wait_ge(tm_mm, NV + n + 1)
                g = 3 + n // 4
                nc.scalar.activation(og[:, n], ps[:, 4 * (g % 2) + n % 4, :], ACT.Silu).then_inc(og_out, 1)
            for q in range(NQ):
                g, k = divmod(q, KD)
                act.wait_ge(tm_in[q % 2], 16 * (q // 2 + 1))
                if q >= 2:
                    g2, k2 = divmod(q - 2, KD)
                    act.wait_ge(*((tm_mm, first_tile[g2 + 1]) if k2 == KD - 1 else (tm_used, q - 2 - g2 + 1)))
                high_part(nc, wt_split[:, q % 2, 0], wt[:, q % 2]).then_inc(tm_high, 1)
                if g == 4 and k in (1, 2, 3, 4):
                    gate(k - 1)

            def split(n):
                act.wait_ge(cm_in, 16 * (n + 1))
                act.wait_ge(*((cm_mm, n - 1) if n >= 2 else (tm_mm, first_tile[-1])))
                high_part(nc, wc_split[:, n % 2, 0], wc[:]).then_inc(cm_high, 1)
            split(0)
            for n in range(4, TT):
                gate(n)
            split(1)
            for n, (kind, _) in enumerate(kinds):
                if n + 2 < NB:
                    split(n + 2)
                if kind == "sc":
                    m = (n - irregular) // 3
                    act.wait_ge(cm_mm, n + 1)
                    if m:
                        act.wait_ge(conv_done, m)
                    nc.scalar.activation(scx[:], flat[:, 0:T], ACT.Copy).then_inc(sc_out, 1)

        @s.b.vector
        def _(dve):
            def value(n):
                dve.wait_ge(tm_mm, n + 1)
                nc.vector.tensor_copy(v[:, n], ps[:, n % 8, :]).then_inc(v_out, 1)
            for q in range(NQ):
                g, k = divmod(q, KD)
                dve.wait_ge(tm_high, q + 1)
                low_part(nc, wt_split[:, q % 2, 1], wt[:, q % 2], wt_split[:, q % 2, 0]).then_inc(tm_low, 1)
                if 1 <= g <= 3 and 1 <= k <= len(groups[g - 1][1]):
                    value(4 * (g - 1) + k - 1)

            def split(n):
                dve.wait_ge(cm_high, n + 1)
                low_part(nc, wc_split[:, n % 2, 1], wc[:], wc_split[:, n % 2, 0]).then_inc(cm_low, 1)
            split(0)
            split(1)
            kept = {"low": (low[:], 2 * LOWR), "k0": (kT[:, 0], P), "k1": (kT[:, 1], P),
                    "q0": (qT[:, 0], P), "q1": (qT[:, 1], P)}
            grid = lambda a, lo, hi: a.rearrange("p (r w) -> p r w", w=GRID_W)[:, :, lo:hi]
            for n, (kind, _) in enumerate(kinds):
                if n < irregular:
                    dst, m = kept[kind]
                    first = CT if kind[0] == "q" else 0
                    dve.wait_ge(cm_mm, n + 1)
                    base = 512 * banks(n) + 256 + first
                    nc.vector.tensor_copy(dst, flat[0:m, base:base + NT * P - first]).then_inc(cm_out, 1)
                if n + 2 < NB:
                    split(n + 2)
                if kind == "sx":
                    m = (n - irregular) // 3
                    conv = osc[:, m]
                    dve.wait_ge(cm_mm, n + 1)
                    dve.wait_ge(sc_out, m + 1)
                    nc.vector.tensor_tensor(scx[:], scx[:], flat[:, 1024:1024 + T], ALU.mult).then_inc(sx_out, 1)
                    dve.wait_ge(sx_out, m + 1)
                    nc.vector.tensor_scalar(conv, scx[:], core.col("w_sc", 4 + m), core.col("b_sc", m),
                                            ALU.mult, ALU.add).then_inc(order, 1)
                    dve.wait_ge(order, 3 * m + 1)
                    nc.vector.scalar_tensor_tensor(out=grid(conv, 1, 64), in0=grid(scx.ap(), 0, 63),
                                                   scalar=core.col("w_sc", m), in1=grid(conv, 1, 64),
                                                   op0=ALU.mult, op1=ALU.add).then_inc(order, 1)
                    dve.wait_ge(order, 3 * m + 2)
                    nc.vector.scalar_tensor_tensor(out=grid(conv, 0, 63), in0=grid(scx.ap(), 1, 64),
                                                   scalar=core.col("w_sc", 8 + m), in1=grid(conv, 0, 63),
                                                   op0=ALU.mult, op1=ALU.add).then_inc(order, 1)
                if kind == "sb":
                    m = (n - irregular) // 3
                    dve.wait_ge(order, 3 * m + 3)
                    dve.wait_ge(cm_mm, n + 1)
                    nc.vector.tensor_tensor(osc[:, m], osc[:, m], flat[:, 2048:2048 + T], ALU.mult
                                            ).then_inc(conv_done, 1)


def stage_gates(core):
    nc, dram, ps = core.nc, core.dram, core.psum
    NT = CTT + TT
    N = NT * P
    flat = ps.ap().rearrange("p b n -> p (b n)")
    qe = core.qe = core.at("q_decayed", 76, [P, 4, T])
    ke = core.ke = core.at("k_grown", 92, [P, 4, N])
    pl = core.pl = core.at("chunk_decay", 10, [P, 4, NT])
    wg = core.at("w_gates", 18, [2 * LOWR, 2, QK])
    e_in = core.at("gate_exp", 12, [P, N])
    soft = core.at("gate_soft", 191, [P, N])
    g = core.at("gate_log", 196, [P, N])
    b = core.at("gate_sum", 201, [P, N])
    reset = core.at("chunk_reset", 36, [P, N])
    with Stage(core, "gates") as s:
        w_in, zeroed, a_mm, a_out, soft_done, order, sum_done, e_done, ei_done, q_done, k_done, read_in = s.sems(
            "w_in", "zeroed", "a_mm", "a_out", "soft_done", "order", "sum_done", "e_done", "ei_done", "q_done",
            "k_done", "read_in")
        soft_order = s.sem("soft_order")

        @s.b.gpsimd
        def _(pool):
            nc.gpsimd.memset(wg[:], 0.0).then_inc(zeroed, 1)
            nc.gpsimd.memset(reset[:], 1.0).then_inc(zeroed, 1)
            pool.wait_ge(zeroed, 2)
            nc.gpsimd.memset(reset.ap().rearrange("p (c t) -> p c t", t=CH)[:, :, 0:1], 0.0).then_inc(zeroed, 1)

        @s.b.sync
        def _(sp):
            sp.wait_ge(zeroed, 1)
            sp.dma_start(wg[0:LOWR, 0, :], dram["w_af"][0]).then_inc(w_in, 16)
            sp.dma_start(wg[LOWR:2 * LOWR, 1, :], dram["w_ab"][0]).then_inc(w_in, 16)

        @s.b.tensor
        def _(pe):
            pe.wait_ge(w_in, 32)
            for u in range(4):
                if u >= 2:
                    pe.wait_ge(a_out, 2 * u - 2)
                d, p = divmod(u, 2)
                for a, (t0, tn) in enumerate(((0, CT), (CT, 512), (CT + 512, 512))):
                    ins = nc.tensor.matmul(ps[:, 4 * (u % 2) + a, 512 - tn:512], wg[:, d, p * P:(p + 1) * P],
                                           core.low[:, t0:t0 + tn], start=True, stop=True)
                ins.then_inc(a_mm, 1)

        def gate_bias(u):
            return core.col(("b_af", "b_ab")[u // 2], u % 2)

        @s.b.scalar
        def _(act):
            nc.scalar.preload_act_table_set("natural_log_exp_and_others")
            for u in range(4):
                a = flat[:, 2048 * (u % 2) + 256:2048 * (u % 2) + 256 + N]
                act.wait_ge(a_mm, u + 1)
                if u >= 1:
                    act.wait_ge(order, u)
                nc.scalar.activation(soft[:], a, ACT.Abs, bias=gate_bias(u)).then_inc(a_out, 1)
                act.wait_ge(a_out, 2 * u + 1)
                nc.scalar.activation(soft[:], soft[:], ACT.Exp, scale=-1.0).then_inc(soft_order, 1)
                act.wait_ge(soft_order, u + 1)
                nc.scalar.activation(soft[:], soft[:], ACT.Ln, bias=1.0).then_inc(soft_done, 1)
                act.wait_ge(sum_done, u + 1)
                if u >= 1:
                    act.wait_ge(read_in, 2 * u)
                nc.scalar.activation(e_in[:], b[:], ACT.Exp, scale=1.0 / TAU).then_inc(e_done, 1)
                act.wait_ge(read_in, 2 * u + 1)
                act.wait_ge(e_done, u + 1)
                nc.scalar.activation(e_in[:], b[:], ACT.Exp, scale=-1.0 / TAU).then_inc(ei_done, 1)

        @s.b.vector
        def _(dve):
            dve.wait_ge(zeroed, 3)
            for u in range(4):
                d, p = divmod(u, 2)
                a = flat[:, 2048 * (u % 2) + 256:2048 * (u % 2) + 256 + N]
                dve.wait_ge(a_out, 2 * u + 1)
                if u >= 1:
                    dve.wait_ge(sum_done, u)
                nc.vector.tensor_scalar(g[:], a, gate_bias(u), 0.0, ALU.add, ALU.min).then_inc(a_out, 1)
                dve.wait_ge(soft_done, u + 1)
                dve.wait_ge(a_out, 2 * u + 2)
                nc.vector.tensor_tensor(g[:], g[:], soft[:], ALU.subtract).then_inc(order, 1)
                dve.wait_ge(order, u + 1)
                if u >= 1:
                    dve.wait_ge(ei_done, u)
                scan = nc.vector.tensor_tensor_scan(b[:], reset[:], g[:], 0.0, ALU.mult, ALU.add)
                if d == 0:
                    scan.then_inc(sum_done, 1)
                else:
                    scan.then_inc(q_done, 1)
                    dve.wait_ge(q_done, 1 + 2 * (u - 2))
                    nc.vector.tensor_tensor(g[:], g[:], b[:], ALU.subtract).then_inc(q_done, 1)
                    dve.wait_ge(q_done, 2 + 2 * (u - 2))
                    b3 = b.ap().rearrange("p (c t) -> p c t", t=CH)
                    nc.vector.tensor_tensor(soft.ap().rearrange("p (c t) -> p c t", t=CH),
                                            g.ap().rearrange("p (c t) -> p c t", t=CH),
                                            b3[:, :, CH - 1:CH].to_broadcast([P, NT, CH]), ALU.add).then_inc(k_done, 1)
                    dve.wait_ge(k_done, u - 1)
                    nc.vector.tensor_copy(b[:], soft[:]).then_inc(sum_done, 1)
                dve.wait_ge(e_done, u + 1)
                end = CH - 1 if d == 0 else 0
                nc.vector.tensor_copy(pl[:, u, :], e_in.ap().rearrange("p (c t) -> p c t", t=CH)[:, :, end])
                nc.vector.scalar_tensor_tensor(out=qe[:, u], in0=core.qT[:, p], scalar=float(DK) ** -0.5,
                                               in1=e_in[:, CT:N], op0=ALU.mult, op1=ALU.mult).then_inc(read_in, 1)
                dve.wait_ge(ei_done, u + 1)
                nc.vector.tensor_tensor(ke[:, u], core.kT[:, p], e_in[:], ALU.mult).then_inc(read_in, 1)


def stage_gla(core):
    nc, ps = core.nc, core.psum
    U, C = range(4), CTT
    qs = core.at("q_chunk", 12, [P, 2, 4, P])
    ks = core.at("k_chunk", 16, [P, 2, 4, P])
    kh = core.at("k_hat", 36, [P, 4, P])
    khT = core.at("k_hat_tm", 38, [P, 4, P])
    att = core.at("scores", 40, [P, 2, 4, P])
    vs = core.at("v_chunk", 112, [P, 2, GV])
    st = core.at("state", 132, [P, 4, DV])
    of = core.of = core.at("out_forward", 191, [P, TT, GV])
    ob = core.ob = core.at("out_backward", 116, [P, TT, GV])
    with Stage(core, "gla") as s:
        zeroed, kh_done, v_staged, qk_staged, turned, khT_done, att_mm, att_done, o_mm, s_mm, s_done, o_out = s.sems(
            "zeroed", "kh_done", "v_staged", "qk_staged", "turned", "khT_done", "att_mm", "att_done", "o_mm", "s_mm",
            "s_done", "o_out")

        def ctx_chunk(n, d):
            return n if d == 0 else CTT - 1 - n

        def x_chunk(i, j, d, first=CTT):
            return (i * 2 + (first + j)) if d == 0 else (i * -2 + (first + TT - 1 - j))

        @s.b.gpsimd
        def _(pool):
            for n in range(C):
                if n:
                    pool.wait_ge(s_mm, n)
                for d in range(2):
                    ins = nc.gpsimd.tensor_copy(vs[:, d], core.v[:, ctx_chunk(n, d), :])
                ins.then_inc(v_staged, 1)

            def step(i, before):
                for j in range(2):
                    pool.wait_ge(s_mm, i * 2 + (C + j))
                    for d in range(2):
                        ins = nc.gpsimd.tensor_copy(vs[:, d:d + 1, :], core.v[:, bass.ds(x_chunk(i, j, d), 1), :])
                    ins.then_inc(v_staged, 1)
            run_loop(pool, TT // 2, step)

        @s.b.scalar
        def _(act):
            def hat(u, cols, n):
                return nc.scalar.activation(kh[:, u], core.ke[:, u, cols], ACT.Copy, scale=core.pl[:, u, n])

            def take_turned():
                nc.scalar.activation(khT[:], ps[:, 2, :].rearrange("p (u t) -> p u t", u=4), ACT.Copy
                                     ).then_inc(khT_done, 1)
            for n in range(C):
                if n:
                    act.wait_ge(turned, n)
                for u in U:
                    c = ctx_chunk(n, u // 2)
                    ins = hat(u, slice(c * P, (c + 1) * P), slice(c, c + 1))
                ins.then_inc(kh_done, 1)
                act.wait_ge(turned, n + 1)
                if n:
                    act.wait_ge(s_mm, n)
                take_turned()

            def step(i, before):
                for j in range(2):
                    act.wait_ge(turned, i * 2 + (C + j))
                    for u in U:
                        c = x_chunk(i, j, u // 2)
                        ins = hat(u, bass.ds(c * P, P), bass.ds(c, 1))
                    ins.then_inc(kh_done, 1)
                    act.wait_ge(turned, i * 2 + (C + j + 1))
                    act.wait_ge(s_mm, i * 2 + (C + j))
                    take_turned()
                    act.wait_ge(o_mm, i * 2 + (j + 1))
                    for d, dst in enumerate((of, ob)):
                        out = dst[:, bass.ds(x_chunk(i, j, d, 0), 1), :].rearrange("p a (u h n) -> p h (a u) n", u=2, h=2)
                        src = ps[:, 3:5, 256 * d:256 * d + 256].rearrange("p h (u n) -> p h u n", u=2)
                        ins = nc.scalar.activation(out, src, ACT.Copy)
                    ins.then_inc(o_out, 1)
            run_loop(act, TT // 2, step)

        @s.b.vector
        def _(dve):
            nc.vector.memset(st[:], 0.0).then_inc(zeroed, 1)
            dve.wait_ge(zeroed, 1)

            def states(decay):
                for u in U:
                    ins = nc.vector.scalar_tensor_tensor(out=st[:, u], in0=st[:, u], scalar=core.pl[:, u, decay(u)],
                                                         in1=ps[:, 5, u * P:(u + 1) * P], op0=ALU.mult, op1=ALU.add)
                ins.then_inc(s_done, 1)
            for n in range(C):
                dve.wait_ge(s_mm, n + 1)
                if n:
                    dve.wait_ge(s_done, n)
                states(lambda u: slice(ctx_chunk(n, u // 2), ctx_chunk(n, u // 2) + 1))

            def step(i, before):
                for j in range(2):
                    if before is not None:
                        dve.wait_ge(o_mm, before * 2 + (j + 1))
                    for d in range(2):
                        uu = slice(2 * d, 2 * d + 2)
                        nc.vector.tensor_copy(qs[:, j, uu], core.qe[:, uu, bass.ds(x_chunk(i, j, d, 0) * P, P)])
                        ins = nc.vector.tensor_copy(ks[:, j, uu], core.ke[:, uu, bass.ds(x_chunk(i, j, d) * P, P)])
                    ins.then_inc(qk_staged, 1)
                    dve.wait_ge(att_mm, i * 2 + (j + 1))
                    if before is not None or j == 1:
                        dve.wait_ge(o_mm, i * 2 + j)
                    for d, m in enumerate((M_UI, M_LS)):
                        for h in range(2):
                            ins = nc.vector.tensor_tensor(
                                att[:, h, 2 * d:2 * d + 2], ps[:, h, 256 * d:256 * d + 256].rearrange(
                                    "p (u t) -> p u t", u=2),
                                core.masks[:, m:m + 1, :].to_broadcast([P, 2, P]), ALU.mult)
                    ins.then_inc(att_done, 1)
                    dve.wait_ge(s_mm, i * 2 + (C + j + 1))
                    dve.wait_ge(s_done, i * 2 + (C + j))
                    states(lambda u: bass.ds(x_chunk(i, j, u // 2), 1))
            run_loop(dve, TT // 2, step)

        @s.b.tensor
        def _(pe):
            def turn():
                for u in U:
                    ins = nc.tensor.transpose(ps[:, 2, u * P:(u + 1) * P], kh[:, u], core.mask(M_ID))
                ins.then_inc(turned, 1)

            def states():
                for u in U:
                    for h in range(2):
                        hd = 2 * (u % 2) + h
                        ins = nc.tensor.matmul(ps[64 * h:64 * h + 64, 5, u * P:(u + 1) * P],
                                               khT[:, u, 64 * h:64 * h + 64], vs[:, u // 2, hd * DV:(hd + 1) * DV],
                                               start=True, stop=True)
                ins.then_inc(s_mm, 1)
            for n in range(C):
                pe.wait_ge(kh_done, n + 1)
                if n:
                    pe.wait_ge(khT_done, n)
                turn()
                pe.wait_ge(khT_done, n + 1)
                pe.wait_ge(v_staged, n + 1)
                if n:
                    pe.wait_ge(s_done, n)
                states()

            def step(i, before):
                for j in range(2):
                    pe.wait_ge(qk_staged, i * 2 + (j + 1))
                    if before is not None or j == 1:
                        pe.wait_ge(att_done, i * 2 + j)
                    for u in U:
                        for h in range(2):
                            a = slice(64 * h, 64 * h + 64)
                            ins = nc.tensor.matmul(ps[:, h, u * P:(u + 1) * P], ks[a, j, u], qs[a, j, u],
                                                   start=True, stop=True)
                    ins.then_inc(att_mm, 1)
                    pe.wait_ge(kh_done, i * 2 + (C + j + 1))
                    pe.wait_ge(khT_done, i * 2 + (C + j))
                    turn()
                    pe.wait_ge(att_done, i * 2 + (j + 1))
                    pe.wait_ge(v_staged, i * 2 + (C + j + 1))
                    pe.wait_ge(s_done, i * 2 + (C + j))
                    if before is not None or j == 1:
                        pe.wait_ge(o_out, i * 2 + j)
                    for u in U:
                        for h in range(2):
                            a = slice(64 * h, 64 * h + 64)
                            hd = 2 * (u % 2) + h
                            out = ps[:, 3 + h, u * P:(u + 1) * P]
                            nc.tensor.matmul(out, att[:, h, u], vs[:, u // 2, hd * DV:(hd + 1) * DV],
                                             start=True, stop=False)
                            ins = nc.tensor.matmul(out, qs[a, j, u], st[a, u], start=False, stop=True)
                    ins.then_inc(o_mm, 1)
                    pe.wait_ge(khT_done, i * 2 + (C + j + 1))
                    states()
            run_loop(pe, TT // 2, step)


def stage_gla_out(core):
    nc, ps = core.nc, core.psum
    of, ob, og = core.of, core.ob, core.og
    NG = TT * NH
    oT = core.oT = core.at("gla_out_cm", 76, [P, 4, T])
    gain = core.at("head_gain", 12, [P, DV])
    stat = core.at("head_stat", 13, [P, 3, NG])
    heads = lambda a: a.ap().rearrange("p t (h n) -> p (t h) n", n=DV)
    with Stage(core, "gla_out") as s:
        gain_in, summed, squared, order, rooted, gated, scaled, done, turned, out_done = s.sems(
            "gain_in", "summed", "squared", "order", "rooted", "gated", "scaled", "done", "turned", "out_done")

        @s.b.sync
        def _(sp):
            sp.dma_start(gain[:], dram_row(core.dram["g_head"], DV)).then_inc(gain_in, 16)

        @s.b.gpsimd
        def _(pool):
            pool.wait_ge(gain_in, 16)
            for t in range(TT):
                o = og[:, t].rearrange("p (h n) -> p h n", n=DV)
                nc.gpsimd.tensor_tensor(o, o, gain.ap().unsqueeze(1).to_broadcast([P, NH, DV]), ALU.mult
                                        ).then_inc(gated, 1)

        @s.b.scalar
        def _(act):
            nc.scalar.preload_act_table(ACT.Sqrt)
            for h in range(2):
                act.wait_ge(summed, h + 1)
                nc.scalar.activation(ob[:, 4 * h:4 * h + 4], of[:, 4 * h:4 * h + 4], ACT.Square).then_inc(squared, 1)
            act.wait_ge(order, 3)
            nc.scalar.activation(stat[:, 2], stat[:, 1], ACT.Sqrt).then_inc(rooted, 1)
            for t in range(TT):
                act.wait_ge(turned, t + 1)
                nc.scalar.activation(oT[:, :, t * P:(t + 1) * P], ps[:, t % 4, :].rearrange("p (c t) -> p c t", c=4),
                                     ACT.Copy).then_inc(out_done, 1)

        @s.b.vector
        def _(dve):
            for h in range(2):
                a = slice(4 * h, 4 * h + 4)
                nc.vector.tensor_tensor(of[:, a], of[:, a], ob[:, a], ALU.add).then_inc(summed, 1)
            for h in range(2):
                dve.wait_ge(squared, h + 1)
                nc.vector.reduce_sum(stat[:, 0, h * NG // 2:(h + 1) * NG // 2],
                                     heads(ob)[:, h * NG // 2:(h + 1) * NG // 2], axis=AX).then_inc(order, 1)
            dve.wait_ge(order, 2)
            nc.vector.tensor_scalar(stat[:, 1], stat[:, 0], 1.0 / DV, EPS, ALU.mult, ALU.add).then_inc(order, 1)
            dve.wait_ge(rooted, 1)
            nc.vector.reciprocal(stat[:, 0], stat[:, 2]).then_inc(order, 1)
            dve.wait_ge(order, 4)
            for t in range(TT):
                dve.wait_ge(gated, t + 1)
                o = of[:, t].rearrange("p (h n) -> p h n", n=DV)
                r = stat[:, 0, NH * t:NH * t + NH].unsqueeze(2).to_broadcast([P, NH, DV])
                g = og[:, t].rearrange("p (h n) -> p h n", n=DV)
                nc.vector.tensor_tensor(g, g, r, ALU.mult).then_inc(scaled, 1)
                dve.wait_ge(scaled, t + 1)
                nc.vector.tensor_tensor(o, o, g, ALU.mult).then_inc(done, 1)

        @s.b.tensor
        def _(pe):
            for t in range(TT):
                pe.wait_ge(done, t + 1)
                if t >= 4:
                    pe.wait_ge(out_done, t - 3)
                for c in range(4):
                    ins = nc.tensor.transpose(ps[:, t % 4, c * P:(c + 1) * P], of[:, t, c * P:(c + 1) * P],
                                              core.mask(M_ID))
                ins.then_inc(turned, 1)


def dram_row(a, n):
    return a.to_broadcast([P, n])


def stage_into_stream(core, name, blocks, lhs, w, ring_kb, split_kb, lhs_kb, scratch_kb, x, x_from,
                      gate_row=None, store=None):
    nc, ps = core.nc, core.psum
    NS, G = 4, 4
    total = (TT // G) * blocks
    ring = core.at(f"{name}_ring", ring_kb, [P, NS, D])
    w_split = core.at(f"{name}_w_split", split_kb, [P, 2, 2, D], F32R)
    l_split = core.at(f"{name}_lhs_split", lhs_kb, [P, 2, 2, G * P], F32R)
    junk = core.at(f"{name}_junk", scratch_kb, [P, D])
    y = core.at(f"{name}_y", scratch_kb + 4, [P, D])
    stat = core.at(f"{name}_stat", 10.25, [P, 3, TT])
    x_rows = x_from.rearrange("(t p) d -> p t d", p=P)
    with Stage(core, name) as s:
        w_in = [s.sem(f"w_in{n}") for n in range(NS)]
        x_in, high, low, used, y_mm, squared, order, rooted, taken, added, stored = s.sems(
            "x_in", "high", "low", "used", "y_mm", "squared", "order", "rooted", "taken", "added", "stored")

        @s.b.sync
        def _(sp):
            def keep(t):
                sp.wait_ge(added if gate_row is not None else taken, t + 1)
                sp.dma_start(store[t * P:(t + 1) * P, :], x[:, t]).then_inc(stored, 16)
            for q in range(total):
                if q >= NS:
                    sp.wait_ge(low, q - NS + 1)
                k = q % blocks
                sp.dma_start(ring[:, q % NS], w[k * P:(k + 1) * P, :]).then_inc(w_in[q % NS], 16)
                if q == NS - 1:
                    sp.dma_start(x[:], x_rows).then_inc(x_in, 16)
            if store is not None:
                for t in range(TT):
                    keep(t)
                sp.wait_ge(stored, 16 * TT)

        @s.b.tensor
        def _(pe):
            for q in range(total):
                g, k = divmod(q, blocks)
                pe.wait_ge(low, q + 1)
                for n in range(G):
                    if k == 0 and g > 0:
                        pe.wait_ge(taken, g * G + n - G + 1)
                    for h in range(2):
                        ins = split_product(nc, ps[:, 2 * n + h, :],
                                            [l_split[:, q % 2, m, n * P:(n + 1) * P] for m in range(2)],
                                            [w_split[:, q % 2, m, 512 * h:512 * h + 512] for m in range(2)],
                                            k == 0, k == blocks - 1)
                    if k == blocks - 1:
                        ins.then_inc(y_mm, 1)
                if k < blocks - 1:
                    ins.then_inc(used, 1)

        def product(t):
            return ps[:, 2 * (t % G):2 * (t % G) + 2, :].rearrange("p b n -> p (b n)")

        def with_splits(split, out):
            for q in range(total):
                split(q)
                g, k = divmod(q, blocks)
                if g and k == 0:
                    out(g - 1)
            out(TT // G - 1)

        @s.b.scalar
        def _(act):
            nc.scalar.preload_act_table(ACT.Sqrt)

            def split(q):
                g, k = divmod(q, blocks)
                act.wait_ge(w_in[q % NS], 16 * (q // NS + 1))
                if q >= 2:
                    g2, k2 = divmod(q - 2, blocks)
                    act.wait_ge(*((y_mm, (g2 + 1) * G) if k2 == blocks - 1 else (used, q - 2 - g2 + 1)))
                high_part(nc, w_split[:, q % 2, 0], ring[:, q % NS])
                high_part(nc, l_split[:, q % 2, 0], lhs(k, g)).then_inc(high, 1)

            def root(t):
                act.wait_ge(order, 2 * t + 1)
                nc.scalar.activation(stat[:, 2, t:t + 1], stat[:, 1, t:t + 1], ACT.Sqrt).then_inc(rooted, 1)

            def out(g):
                if gate_row is None:
                    return
                for t in range(g * G, g * G + G):
                    act.wait_ge(y_mm, t + 1)
                    if t:
                        act.wait_ge(squared, t)
                    nc.scalar.activation(junk[:], product(t), ACT.Square, accum_out=stat[:, 0, t:t + 1]
                                         ).then_inc(squared, 1)
                    if t > g * G:
                        root(t - 1)
                root(g * G + G - 1)
            with_splits(split, out)

        if gate_row is not None:
            @s.b.gpsimd
            def _(pool):
                pool.wait_ge(x_in, 16)
                for t in range(TT):
                    pool.wait_ge(taken, t + 1)
                    nc.gpsimd.tensor_tensor(x[:, t], x[:, t], y[:], ALU.add).then_inc(added, 1)

        @s.b.vector
        def _(dve):
            def split(q):
                g, k = divmod(q, blocks)
                dve.wait_ge(high, q + 1)
                low_part(nc, w_split[:, q % 2, 1], ring[:, q % NS], w_split[:, q % 2, 0])
                low_part(nc, l_split[:, q % 2, 1], lhs(k, g), l_split[:, q % 2, 0]).then_inc(low, 1)

            def out(g):
                for t in range(g * G, g * G + G):
                    if gate_row is None:
                        dve.wait_ge(y_mm, t + 1)
                        dve.wait_ge(x_in, 16)
                        nc.vector.tensor_tensor(x[:, t], x[:, t], product(t), ALU.add).then_inc(taken, 1)
                        continue
                    dve.wait_ge(squared, t + 1)
                    nc.vector.tensor_scalar(stat[:, 1, t:t + 1], stat[:, 0, t:t + 1], 1.0 / D, EPS, ALU.mult, ALU.add
                                            ).then_inc(order, 1)
                    dve.wait_ge(rooted, t + 1)
                    nc.vector.reciprocal(stat[:, 0, t:t + 1], stat[:, 2, t:t + 1]).then_inc(order, 1)
                    dve.wait_ge(order, 2 * t + 2)
                    if t:
                        dve.wait_ge(added, t)
                    nc.vector.scalar_tensor_tensor(out=y[:], in0=product(t), scalar=stat[:, 0, t:t + 1], in1=gate_row,
                                                   op0=ALU.mult, op1=ALU.mult).then_inc(taken, 1)
            with_splits(split, out)


def stage_ffn_up(core, hT):
    nc, dram, ps = core.nc, core.dram, core.psum
    flat = ps.ap().rearrange("p b n -> p (b n)")
    w_up = dram["w_up"][0]
    GH, GW = GRID_H + 2, GRID_W + 2
    ff = core.ff = core.at("ffn_hidden", 44, [P, FB, T])
    wr = [core.at(f"w_raw{m}", kb, [P, KD, P]) for m, kb in enumerate((12, 16))]
    wh, wl = ([core.at(f"w_{part}{m}", kb, [P, KD, P], F32R) for m, kb in enumerate(kbs)]
              for part, kbs in (("high", (20, 36)), ("low", (24, 40))))
    pad = [core.at(f"u_padded{j}", 196 + 5 * j, [P, GH, GW]) for j in range(2)]
    block = lambda n: ff[:, bass.ds(n, 1), :].rearrange("p a t -> p (a t)")
    with Stage(core, "ffn_up") as s:
        w_in = [s.sem(f"w_in{m}") for m in range(2)]
        high = [s.sem(f"high{m}") for m in range(2)]
        low = [s.sem(f"low{m}") for m in range(2)]
        zeroed, u_mm, g_mm, u_out, order, conv_done, silu_done, ff_done = s.sems(
            "zeroed", "u_mm", "g_mm", "u_out", "order", "conv_done", "silu_done", "ff_done")
        sides = ((0, u_mm), (1, g_mm))

        @s.b.sync
        def _(sp):
            def load(i, before):
                for j in range(2):
                    for m, (side, _) in enumerate(sides):
                        if before is not None or j:
                            sp.wait_ge(low[m], i * 2 + j)
                        sp.dma_start(wr[m][:], weight_columns(w_up, i * 256 + (FF * side + 128 * j), P)
                                     ).then_inc(w_in[m], 16)
            run_loop(sp, FB // 2, load)

        @s.b.tensor
        def _(pe):
            def products(i, before):
                for j in range(2):
                    for m, (side, done) in enumerate(sides):
                        pe.wait_ge(low[m], i * 2 + (j + 1))
                        if before is not None:
                            pe.wait_ge((u_out, ff_done)[side], before * 2 + (j + 1))
                        for h in range(2):
                            for k in range(KD):
                                ins = split_product(nc, ps[:, 4 * j + 2 * side + h, :], (wh[m][:, k], wl[m][:, k]),
                                                    [a[:, k, 512 * h:512 * h + 512] for a in hT],
                                                    k == 0, k == KD - 1)
                        ins.then_inc(done, 1)
            run_loop(pe, FB // 2, products)

        @s.b.gpsimd
        def _(pool):
            for j in range(2):
                nc.gpsimd.memset(pad[j][:], 0.0).then_inc(zeroed, 1)

        @s.b.scalar
        def _(act):
            nc.scalar.preload_act_table(ACT.Silu)
            act.wait_ge(zeroed, 2)

            def work(i, before):
                for j in range(2):
                    for m, (side, done) in enumerate(sides):
                        act.wait_ge(w_in[m], i * 32 + (16 * j + 16))
                        if before is not None or j:
                            act.wait_ge(done, i * 2 + j)
                        high_part(nc, wh[m][:], wr[m][:]).then_inc(high[m], 1)
                        if m == 0 and (before is not None or j):
                            into_pad(i, before, j)
                    if before is not None or j:
                        silu(i, before, j)

            def into_pad(i, before, j):
                p = 1 - j
                act.wait_ge(u_mm, i * 2 + j)
                nc.scalar.activation(pad[p][:, 1:GH - 1, 1:GW - 1],
                                     flat[:, 2048 * p:2048 * p + T].rearrange("p (r w) -> p r w", w=GRID_W),
                                     ACT.Copy).then_inc(u_out, 1)

            def silu(i, before, j):
                act.wait_ge(conv_done, i * 2 + j)
                nc.scalar.activation(block(i * 2 + (j - 1)), block(i * 2 + (j - 1)), ACT.Silu).then_inc(silu_done, 1)
            run_loop(act, FB // 2, work)
            into_pad(FB // 2, None, 0)
            silu(FB // 2, None, 0)

        @s.b.vector
        def _(dve):
            def split(i, before, j, m):
                dve.wait_ge(high[m], i * 2 + (j + 1))
                low_part(nc, wl[m][:], wr[m][:], wh[m][:]).then_inc(low[m], 1)

            def conv(i, before, j):
                n, p = i * 2 + (j - 1), 1 - j
                dve.wait_ge(u_out, i * 2 + j)
                for tap in range(9):
                    r, c = divmod(tap, 3)
                    src = pad[p][:, r:r + GRID_H, c:c + GRID_W]
                    out = block(n).rearrange("p (r w) -> p r w", w=GRID_W)
                    weight = core.pcol[:, bass.ds(n + (PCOL["w_cf"] + FB * tap), 1)]
                    if tap == 0:
                        ins = nc.vector.tensor_scalar(out, src, weight, core.pcol[:, bass.ds(n + PCOL["b_cf"], 1)],
                                                      ALU.mult, ALU.add)
                    else:
                        dve.wait_ge(order, i * 16 + (8 * (j - 1) + tap))
                        ins = nc.vector.scalar_tensor_tensor(out=out, in0=src, scalar=weight, in1=out,
                                                             op0=ALU.mult, op1=ALU.add)
                    ins.then_inc(order if tap < 8 else conv_done, 1)

            def gated(i, before, j):
                n, p = i * 2 + (j - 1), 1 - j
                dve.wait_ge(silu_done, i * 2 + j)
                dve.wait_ge(g_mm, i * 2 + j)
                nc.vector.tensor_tensor(block(n), block(n), flat[:, 2048 * p + 1024:2048 * p + 1024 + T], ALU.mult
                                        ).then_inc(ff_done, 1)

            def work(i, before):
                for j in range(2):
                    split(i, before, j, 0)
                    split(i, before, j, 1)
                    if before is not None or j:
                        conv(i, before, j)
                        gated(i, before, j)
            run_loop(dve, FB // 2, work)
            conv(FB // 2, None, 0)
            gated(FB // 2, None, 0)


def first_block(core):
    dram = core.dram
    stage_modulation(core)
    rows = core.rows
    core.hT_x = (core.at("mix_x_high", 84, [P, KD, T], F32R), core.at("mix_x_low", 44, [P, KD, T], F32R))
    core.hT_ctx = (core.at("mix_ctx_high", 76, [P, KD, CT], F32R), core.at("mix_ctx_low", 12, [P, KD, CT], F32R))
    stage_norm_turn(core, "norm1", [(core.x0, TT, rows[:, R_G1], rows[:, R_SH1], core.hT_x, 0),
                                    (core.ctx, CTT, rows[:, R_CG], rows[:, R_CSH], core.hT_ctx, 0)], 150)
    stage_project_mix(core)
    stage_gates(core)
    stage_gla(core)
    stage_gla_out(core)
    stage_into_stream(core, "mix_out", 8,
                      lambda k, g: (core.oT[:, k] if k < 4 else core.osc[:, k - 4])[:, g * 512:g * 512 + 512],
                      dram["w_out"][0], 92, 108, 124, 191, core.x, dram["x"][0], rows[:, R_GP1], dram["stream"])
    core.hT2 = (core.at("ffn_high", 132, [P, KD, T], F32R), core.at("ffn_low", 164, [P, KD, T], F32R))
    stage_norm_turn(core, "norm2", [(core.x, TT, rows[:, R_G2], rows[:, R_SH2], core.hT2, 0)], 80)
    stage_ffn_up(core, core.hT2)
    core.x2 = core.at("x_after_ffn", 132, [P, TT, D])
    stage_into_stream(core, "ffn_down", FB, lambda k, g: core.ff[:, k, g * 512:g * 512 + 512],
                      dram["w_down"][0], 164, 180, 12, 196, core.x2, dram["stream"], rows[:, R_GP2], dram["stream"])


def stage_attention_project(core, hT):
    nc, dram, ps = core.nc, core.dram, core.psum
    flat = ps.ap().rearrange("p b n -> p (b n)")
    w = dram["w_in_2"][0]
    q = core.q = core.at("att_q", 108, [P, 4, T])
    kd = core.kd = core.at("att_k_twice", 124, [P, AKV, T + 2 * P])
    v = core.av = core.at("att_v", 134, [P, TT + 2, AKV * ADH])
    slots = [core.at(f"w_att{n}", 151 + 4 * n, [P, KD, P]) for n in range(4)]
    wv = core.at("w_att_v", 167, [P, KD, P])
    with Stage(core, "att_in") as s:
        w_in = [s.sem(f"w_in{n}") for n in range(4)]
        wv_in, mm, out, v_mm, v_out, padded = s.sems("wv_in", "mm", "out", "v_mm", "v_out", "padded")
        NB = 6

        @s.b.sync
        def _(sp):
            for n in range(NB):
                if n >= 4:
                    sp.wait_ge(mm, n - 3)
                if n < 4:
                    sp.dma_start(slots[n][:], weight_columns(w, C2_Q + n * P, P)).then_inc(w_in[n], 16)
                else:
                    for h in range(2):
                        sp.dma_start(slots[n % 4][:, :, 64 * h:64 * h + 64],
                                     weight_columns(w, C2_K + 64 * (n - 4), 64)).then_inc(w_in[n % 4], 16)
            sp.dma_start(wv[:], weight_columns(w, C2_V, P)).then_inc(wv_in, 16)

        @s.b.tensor
        def _(pe):
            for n in range(NB):
                pe.wait_ge(w_in[n % 4], 16 if n < 4 else 48)
                if n >= 4:
                    pe.wait_ge(out, n - 3)
                for h in range(2):
                    for k in range(KD):
                        ins = nc.tensor.matmul(ps[:, 2 * (n % 4) + h, :], slots[n % 4][:, k],
                                               hT[:, k, 512 * h:512 * h + 512], start=(k == 0), stop=(k == KD - 1))
                ins.then_inc(mm, 1)
            pe.wait_ge(wv_in, 16)
            pe.wait_ge(out, NB)
            for t in range(TT):
                for k in range(KD):
                    ins = nc.tensor.matmul(ps[:, t, 0:P], hT[:, k, t * P:(t + 1) * P], wv[:, k],
                                           start=(k == 0), stop=(k == KD - 1))
                ins.then_inc(v_mm, 1)

        @s.b.gpsimd
        def _(pool):
            nc.gpsimd.memset(kd[:, :, 0:P], 0.0)
            nc.gpsimd.memset(kd[:, :, P + T:], 0.0)
            nc.gpsimd.memset(v[:, 0], 0.0)
            nc.gpsimd.memset(v[:, TT + 1], 0.0).then_inc(padded, 1)

        @s.b.scalar
        def _(act):
            for n in range(NB):
                act.wait_ge(mm, n + 1)
                dst, scale = (q[:, n], ADH ** -0.5) if n < 4 else (kd[:, n - 4, P:P + T], 1.0)
                nc.scalar.activation(dst, flat[:, 1024 * (n % 4):1024 * (n % 4) + T], ACT.Copy, scale=scale
                                     ).then_inc(out, 1)

        @s.b.vector
        def _(dve):
            for t in range(TT):
                dve.wait_ge(v_mm, t + 1)
                nc.vector.tensor_copy(v[:, t + 1], ps[:, t, 0:P]).then_inc(v_out, 1)


def stage_attention(core):
    nc, dram, ps = core.nc, core.dram, core.psum
    H, SP = 4, 3 * P
    bias = core.at("alibi", 139, [P, AH, SP])
    qs = core.at("q_padded", 151, [P, 2, 4, P])
    sc = core.at("scores_sb", 155, [P, 2, H, SP])
    pT = core.at("probs_turned", 167, [P, H, 3, P])
    y = core.at("att_out", 173, [P, 2, 512])
    sink = core.at("sink", 177, [P, AH])
    stat = core.at("softmax_stat", 177.25, [P, 2, 6, H])
    yT = core.yaT = core.at("att_out_cm", 12, [P, 4, T])
    MX, NM, RS, ES, DEN, SM = range(6)
    with Stage(core, "att") as s:
        (bias_in, sink_in, zeroed, q_staged, s_mm, s_added, max_done, sink_sub, exp_done, den_done, turned,
         pT_done, o_mm, y_done, y_turned, yT_out, order) = s.sems(
            "bias_in", "sink_in", "zeroed", "q_staged", "s_mm", "s_added", "max_done", "sink_sub", "exp_done",
            "den_done", "turned", "pT_done", "o_mm", "y_done", "y_turned", "yT_out", "order")

        def blocks(eng, body):
            body(0, None, 0)
            with eng.Fori(0, TT - 2) as before:
                body(before + 1, before, None)
            body(TT - 1, TT - 2, 2)

        @s.b.sync
        def _(sp):
            sp.dma_start(bias[:], dram["alibi"]).then_inc(bias_in, 16)
            sp.dma_start(sink[:], dram["attn_sink_2"].to_broadcast([P, AH])).then_inc(sink_in, 16)

        @s.b.gpsimd
        def _(pool):
            nc.gpsimd.memset(qs[:], 0.0).then_inc(zeroed, 1)
            pool.wait_ge(zeroed, 1)

            def stage(i, before, edge):
                for g in range(2):
                    if before is not None:
                        pool.wait_ge(s_mm, before * 2 + (g + 1))
                    for h in range(2):
                        a = slice(64 * h, 64 * h + 64)
                        ins = nc.gpsimd.tensor_copy(qs[a, g, h:4:2], core.q[a, 2 * g:2 * g + 2, bass.ds(i * P, P)])
                    ins.then_inc(q_staged, 1)
            blocks(pool, stage)

        @s.b.tensor
        def _(pe):
            def work(i, before, edge):
                for g in range(2):
                    pe.wait_ge(q_staged, i * 2 + (g + 1))
                    if before is not None or g:
                        pe.wait_ge(s_added, i * 2 + g)
                    for h in range(H):
                        ins = nc.tensor.matmul(ps[:, h, 0:SP], qs[:, g, h], core.kd[:, g, bass.ds(i * P, SP)],
                                               start=True, stop=True)
                    ins.then_inc(s_mm, 1)
                for g in range(2):
                    pe.wait_ge(exp_done, i * 2 + (g + 1))
                    for h in range(H):
                        if before is not None or g or h >= 2:
                            pe.wait_ge(pT_done, i * 8 + (4 * g + h - 1))
                        for b in range(3):
                            ins = nc.tensor.transpose(ps[:, 4 + h % 2, b * P:(b + 1) * P],
                                                      sc[:, g, h, b * P:(b + 1) * P], core.mask(M_ID))
                        ins.then_inc(turned, 1)
                    if before is not None or g:
                        pe.wait_ge(y_done, i * 2 + g)
                    for h in range(H):
                        pe.wait_ge(pT_done, i * 8 + (4 * g + h + 1))
                        for b in range(3):
                            ins = nc.tensor.matmul(ps[:, 6, h * ADH:(h + 1) * ADH], pT[:, h, b],
                                                   core.av[:, bass.ds(i + b, 1), g * ADH:(g + 1) * ADH],
                                                   start=(b == 0), stop=(b == 2))
                    ins.then_inc(o_mm, 1)
                pe.wait_ge(y_done, i * 2 + 2)
                if before is not None:
                    pe.wait_ge(yT_out, before + 1)
                for c in range(4):
                    ins = nc.tensor.transpose(ps[:, 7, c * P:(c + 1) * P], y[:, 0, c * P:(c + 1) * P],
                                              core.mask(M_ID))
                ins.then_inc(y_turned, 1)
            pe.wait_ge(zeroed, 1)
            blocks(pe, work)

        @s.b.scalar
        def _(act):
            nc.scalar.preload_act_table(ACT.Exp)

            def work(i, before, edge):
                for g in range(2):
                    act.wait_ge(sink_sub, i * 2 + (g + 1))
                    for h in range(H):
                        nc.scalar.activation(sc[:, g, h], sc[:, g, h], ACT.Exp, bias=stat[:, g, NM, h:h + 1],
                                             accum_out=stat[:, g, RS, h:h + 1])
                    nc.scalar.activation(stat[:, g, ES], stat[:, g, SM], ACT.Exp).then_inc(exp_done, 1)
                for g in range(2):
                    for h in range(1, H, 2):
                        act.wait_ge(turned, i * 8 + (4 * g + h + 1))
                        if before is not None or g:
                            act.wait_ge(o_mm, i * 2 + g)
                        act.wait_ge(pT_done, i * 8 + (4 * g + h))
                        nc.scalar.activation(pT[:, h], ps[:, 5, 0:SP].rearrange("p (b t) -> p b t", b=3),
                                             ACT.Copy).then_inc(pT_done, 1)
                act.wait_ge(y_turned, i + 1)
                nc.scalar.activation(yT[:, :, bass.ds(i * P, P)], ps[:, 7, :].rearrange("p (c t) -> p c t", c=4),
                                     ACT.Copy).then_inc(yT_out, 1)
            blocks(act, work)

        @s.b.vector
        def _(dve):
            dve.wait_ge(bias_in, 16)
            dve.wait_ge(sink_in, 16)

            def work(i, before, edge):
                for g in range(2):
                    dve.wait_ge(s_mm, i * 2 + (g + 1))
                    if before is not None:
                        dve.wait_ge(turned, before * 8 + (4 * g + 4))
                    nc.vector.tensor_tensor(sc[:, g], ps[:, 0:4, 0:SP], bias[:, 4 * g:4 * g + 4, :], ALU.add
                                            ).then_inc(s_added, 1)
                    dve.wait_ge(s_added, i * 2 + (g + 1))
                    extra = 0 if edge is None else 1
                    at = i * 8 + (4 * g + (0 if before is None else 2) + (g if extra else 0))
                    if extra:
                        nc.vector.memset(sc[:, g, :, edge * P:(edge + 1) * P], NEG).then_inc(order, 1)
                        dve.wait_ge(order, at + 1)
                    nc.vector.reduce_max(stat[:, g, MX], sc[:, g], axis=AX).then_inc(order, 1)
                    dve.wait_ge(order, at + extra + 1)
                    nc.vector.tensor_tensor(stat[:, g, MX], stat[:, g, MX], sink[:, 4 * g:4 * g + 4], ALU.max
                                            ).then_inc(order, 1)
                    dve.wait_ge(order, at + extra + 2)
                    nc.vector.tensor_scalar(stat[:, g, NM], stat[:, g, MX], -1.0, None, ALU.mult).then_inc(order, 1)
                    nc.vector.tensor_tensor(stat[:, g, SM], sink[:, 4 * g:4 * g + 4], stat[:, g, MX], ALU.subtract
                                            ).then_inc(sink_sub, 1)
                    dve.wait_ge(exp_done, i * 2 + (g + 1))
                    nc.vector.tensor_tensor(stat[:, g, DEN], stat[:, g, RS], stat[:, g, ES], ALU.add
                                            ).then_inc(order, 1)
                    dve.wait_ge(order, at + extra + 4)
                    nc.vector.reciprocal(stat[:, g, DEN], stat[:, g, DEN]).then_inc(den_done, 1)
                for g in range(2):
                    for h in range(0, H, 2):
                        dve.wait_ge(turned, i * 8 + (4 * g + h + 1))
                        if before is not None or g:
                            dve.wait_ge(o_mm, i * 2 + g)
                        if before is not None or g or h:
                            dve.wait_ge(pT_done, i * 8 + (4 * g + h))
                        nc.vector.tensor_copy(pT[:, h], ps[:, 4, 0:SP].rearrange("p (b t) -> p b t", b=3)
                                              ).then_inc(pT_done, 1)
                    dve.wait_ge(o_mm, i * 2 + (g + 1))
                    dve.wait_ge(den_done, i * 2 + (g + 1))
                    if before is not None and g == 0:
                        dve.wait_ge(y_turned, before + 1)
                    nc.vector.tensor_tensor(y[:, 0, 256 * g:256 * g + 256].rearrange("p (h n) -> p h n", h=H),
                                            ps[:, 6, 0:256].rearrange("p (h n) -> p h n", h=H),
                                            stat[:, g, DEN].unsqueeze(2).to_broadcast([P, H, ADH]), ALU.mult
                                            ).then_inc(y_done, 1)
            blocks(dve, work)


def shifted(dst, src, core, block, act, dve, got, half, done, n):
    nc = core.nc

    def on_scalar():
        nc.scalar.activation(dst, src, ACT.Copy, scale=core.keep[:, bass.ds(block, 1)]).then_inc(got, 1)

    def on_vector():
        dve.wait_ge(got, n + 1)
        nc.vector.scalar_tensor_tensor(out=dst[:, 1:T], in0=src[:, 0:T - 1],
                                       scalar=core.pcol[:, bass.ds(block + PCOL["mu_prev_2"], 1)],
                                       in1=dst[:, 1:T], op0=ALU.mult, op1=ALU.add).then_inc(half, 1)
        dve.wait_ge(half, n + 1)
        nc.vector.scalar_tensor_tensor(out=dst[:, 0:T - 1], in0=src[:, 1:T],
                                       scalar=core.pcol[:, bass.ds(block + PCOL["mu_next_2"], 1)],
                                       in1=dst[:, 0:T - 1], op0=ALU.mult, op1=ALU.add).then_inc(done, 1)
    return on_scalar, on_vector


def stage_rwkv_low(core, hT):
    nc, dram, ps = core.nc, core.dram, core.psum
    flat = ps.ap().rearrange("p b n -> p (b n)")
    low = core.lows = core.at("rwkv_low", 124, [P, 3, T])
    core.keep = core.at("shift_keep", 10, [P, 16])
    core.one_ka = core.at("one_minus_ka", 10.0625, [P, 4])
    core.yrT = core.at("rwkv_out_cm", 108, [P, 4, T])
    m4 = core.mask4 = core.at("mask_products", 136, [P, 2, 4, P])
    reset = core.reset = core.at("scan_reset", 140, [P, 2, T])
    w = [core.at(f"w_low{n}", 44 + 4 * n, [P, KD, P]) for n in range(3)]
    with Stage(core, "low") as s:
        w_in = [s.sem(f"w_in{n}") for n in range(3)]
        keep_half, keep_done, mm, got, half, shift, act_done, const_done, ones_done = s.sems(
            "keep_half", "keep_done", "mm", "got", "half", "shift", "act_done", "const_done", "ones_done")
        funcs = (ACT.Sigmoid, ACT.Tanh, None)
        parts = [shifted(low[:, n], flat[:, 1024 * n:1024 * n + T], core, 12 + n, nc.scalar, nc.vector,
                         got, half, shift, n) for n in range(3)]

        @s.b.sync
        def _(sp):
            for n in range(3):
                sp.dma_start(w[n][:], weight_columns(dram["w_in_2"][0], (12 + n) * P, P)).then_inc(w_in[n], 16)

        @s.b.tensor
        def _(pe):
            for n in range(3):
                pe.wait_ge(w_in[n], 16)
                for h in range(2):
                    for k in range(KD):
                        ins = nc.tensor.matmul(ps[:, 2 * n + h, :], w[n][:, k], hT[:, k, 512 * h:512 * h + 512],
                                               start=(k == 0), stop=(k == KD - 1))
                ins.then_inc(mm, 1)

        @s.b.scalar
        def _(act):
            act.wait_ge(keep_done, 1)
            for n in range(3):
                act.wait_ge(mm, n + 1)
                parts[n][0]()
            for n in range(2):
                act.wait_ge(shift, n + 1)
                nc.scalar.activation(low[:, n], low[:, n], funcs[n]).then_inc(act_done, 1)

        @s.b.vector
        def _(dve):
            c = PCOL["mu_prev_2"]
            nc.vector.tensor_tensor(core.keep[:, 0:RB], core.pcol[:, c:c + RB], core.pcol[:, c + RB:c + 2 * RB],
                                    ALU.add).then_inc(keep_half, 1)
            dve.wait_ge(keep_half, 1)
            nc.vector.tensor_scalar(core.keep[:, 0:RB], core.keep[:, 0:RB], -1.0, 1.0, ALU.mult, ALU.add
                                    ).then_inc(keep_done, 1)
            c = PCOL["k_a_2"]
            nc.vector.tensor_scalar(core.one_ka[:], core.pcol[:, c:c + 4], -1.0, 1.0, ALU.mult, ALU.add
                                    ).then_inc(const_done, 1)
            for d, pair in enumerate(((M_US, M_UI), (M_LS, M_LI))):
                for n in range(4):
                    nc.vector.tensor_copy(m4[:, d, n], core.mask(pair[n % 2])).then_inc(const_done, 1)
            for n in range(3):
                parts[n][1]()

        @s.b.gpsimd
        def _(pool):
            nc.gpsimd.memset(reset[:], 1.0).then_inc(ones_done, 1)
            pool.wait_ge(ones_done, 1)
            r = reset.ap().rearrange("p d (c t) -> p d c t", t=CH)
            nc.gpsimd.memset(r[:, 0, :, 0:1], 0.0).then_inc(ones_done, 1)
            nc.gpsimd.memset(r[:, 1, :, CH - 1:CH], 0.0).then_inc(ones_done, 1)


def stage_rwkv_prepare(core, hT, pr):
    nc, dram, ps = core.nc, core.dram, core.psum
    flat = ps.ap().rearrange("p b n -> p (b n)")
    bank2 = lambda n: flat[:, 1024 * n:1024 * n + T]
    src = core.src = core.at("chunk_operands", 148, [P, 2, 4, T])
    vc = core.vc = core.at("v_cm", 180, [P, T])
    bonus = core.bonus = core.at("bonus", 184, [P, T])
    pl = core.pl2 = core.at("pair_chunk_decay", 199, [P, 2, TT])
    w = [core.at(f"w_rkv{n}", 28 + 4 * n, [P, KD, P]) for n in range(3)]
    up = core.at("w_ups", 40, [P, 2, P])
    r, k, kk = (core.at(n, kb, [P, T]) for n, kb in (("r_cm", 44), ("k_cm", 48), ("kk_cm", 52)))
    a = [core.at(f"rate{d}", 56 + 4 * d, [P, T]) for d in range(2)]
    sg = [core.at(f"decay_sigmoid{d}", 64 + 4 * d, [P, T]) for d in range(2)]
    b = [core.at(f"decay_sum{d}", kb, [P, T]) for d, kb in enumerate((72, 188))]
    t1 = core.at("temp1", 192, [P, T])
    e = core.at("decay_exp", 200, [P, T])
    col = lambda name: core.pcol[:, bass.ds(pr + PCOL[name], 1)]
    names = {"w0": ("w0_f_2", "w0_b_2"), "a0": ("a0_f_2", "a0_b_2")}
    with Stage(core, "prep") as s:
        w_in = [s.sem(f"w_in{n}") for n in range(3)]
        up_in, rkv_mm, w_mm, a_mm, got, half, shift, sg_done, a_done = s.sems(
            "up_in", "rkv_mm", "w_mm", "a_mm", "got", "half", "shift", "sg_done", "a_done")
        (sq_done, norm_mm, norm_cut, norm_root, norm_inv, kk_done, scan_done, kd_half, kd_done, akk_done, diff_done,
         bar_exp, bar_used, p_exp, p_used, m_exp, m_used, sum_kd, dots_in, dots_mm, bonus_done, pl_done) = s.sems(
            "sq_done", "norm_mm", "norm_cut", "norm_root", "norm_inv", "kk_done", "scan_done", "kd_half", "kd_done",
            "akk_done", "diff_done", "bar_exp", "bar_used", "p_exp", "p_used", "m_exp", "m_used", "sum_kd",
            "dots_in", "dots_mm", "bonus_done", "pl_done")
        parts = [shifted(dst, bank2(n), core, pr + 4 * n, nc.scalar, nc.vector, got, half, shift, n)
                 for n, dst in enumerate((r[:], k[:], vc[:]))]

        @s.b.sync
        def _(sp):
            for n in range(3):
                sp.dma_start(w[n][:], weight_columns(dram["w_in_2"][0], pr * P + n * RD, P)).then_inc(w_in[n], 16)
            for m, lower in enumerate(("w_up", "a_up")):
                for d, side in enumerate("fb"):
                    sp.dma_start(up[64 * d:64 * d + 64, m], dram[f"{lower}_{side}_2"][0][:, bass.ds(pr * P, P)]
                                 ).then_inc(up_in, 16)

        @s.b.tensor
        def _(pe):
            for n in range(3):
                pe.wait_ge(w_in[n], 16)
                for h in range(2):
                    for kt in range(KD):
                        ins = nc.tensor.matmul(ps[:, 2 * n + h, :], w[n][:, kt], hT[:, kt, 512 * h:512 * h + 512],
                                               start=(kt == 0), stop=(kt == KD - 1))
                ins.then_inc(rkv_mm, 1)
            pe.wait_ge(up_in, 64)
            for n, (m, d, first) in enumerate(((0, 0, 6), (0, 1, 0), (1, 0, 2), (1, 1, 4))):
                if n:
                    pe.wait_ge(shift, n)
                rows = slice(64 * d, 64 * d + 64)
                for h in range(2):
                    ins = nc.tensor.matmul(ps[:, first + h, :], up[rows, m], core.lows[rows, 1 + m, 512 * h:512 * h + 512],
                                           start=True, stop=True)
                ins.then_inc((w_mm, a_mm)[m], 1)
            pe.wait_ge(sq_done, 1)
            pe.wait_ge(sg_done, 1)
            for h in range(2):
                ins = nc.tensor.matmul(ps[:, 6 + h, :], core.mask(M_BO), t1[:, 512 * h:512 * h + 512],
                                       start=True, stop=True)
            ins.then_inc(norm_mm, 1)
            pe.wait_ge(dots_in, 1)
            pe.wait_ge(sg_done, 2)
            for h in range(2):
                ins = nc.tensor.matmul(ps[:, h, :], core.mask(M_BO), t1[:, 512 * h:512 * h + 512],
                                       start=True, stop=True)
            ins.then_inc(dots_mm, 1)

        @s.b.scalar
        def _(act):
            nc.scalar.preload_act_table(ACT.Sigmoid)
            for n in range(3):
                act.wait_ge(rkv_mm, n + 1)
                parts[n][0]()
            act.wait_ge(shift, 2)
            nc.scalar.activation(t1[:], k[:], ACT.Square, scale=col("k_k_2")).then_inc(sq_done, 1)
            for d, first in enumerate((3, 0)):
                act.wait_ge(w_mm, d + 1)
                nc.scalar.activation(sg[d][:], bank2(first), ACT.Sigmoid, bias=col(names["w0"][d])).then_inc(sg_done, 1)
            for d, first in enumerate((1, 2)):
                act.wait_ge(a_mm, d + 1)
                nc.scalar.activation(a[d][:], bank2(first), ACT.Sigmoid, bias=col(names["a0"][d])).then_inc(a_done, 1)
            act.wait_ge(norm_cut, 1)
            nc.scalar.activation(kk[:], kk[:], ACT.Sqrt).then_inc(norm_root, 1)
            for d in range(2):
                act.wait_ge(diff_done, d + 1)
                if d:
                    act.wait_ge(m_used, 1)
                nc.scalar.activation(e[:], src[:, d, 0], ACT.Exp, scale=-DECAY_SCALE).then_inc(bar_exp, 1)
                act.wait_ge(scan_done, d + 1)
                nc.scalar.activation(src[:, d, 1], b[d][:], ACT.Exp, scale=-DECAY_SCALE).then_inc(p_exp, 1)
                act.wait_ge(bar_used, d + 1)
                nc.scalar.activation(e[:], b[d][:], ACT.Exp, scale=DECAY_SCALE).then_inc(m_exp, 1)

        @s.b.gpsimd
        def _(pool):
            for d in range(2):
                pool.wait_ge(scan_done, d + 1)
                nc.gpsimd.tensor_tensor(src[:, d, 0], b[d][:], sg[d][:], ALU.subtract).then_inc(diff_done, 1)
                pool.wait_ge(kk_done, 1)
                pool.wait_ge(a_done, d + 1)
                nc.gpsimd.tensor_tensor(src[:, d, 3], a[d][:], kk[:], ALU.mult).then_inc(akk_done, 1)

        @s.b.vector
        def _(dve):
            for n in range(3):
                parts[n][1]()
            for d in range(2):
                dve.wait_ge(sg_done, d + 1)
                way = slice(None) if d == 0 else slice(None, None, -1)
                nc.vector.tensor_tensor_scan(b[d][:, way], core.reset[:, d, way], sg[d][:, way], 0.0,
                                             ALU.mult, ALU.add).then_inc(scan_done, 1)
            dve.wait_ge(norm_mm, 1)
            nc.vector.tensor_scalar(kk[:], bank2(3), 1e-24, None, ALU.max).then_inc(norm_cut, 1)
            dve.wait_ge(norm_root, 1)
            nc.vector.reciprocal(kk[:], kk[:]).then_inc(norm_inv, 1)
            dve.wait_ge(norm_inv, 1)
            nc.vector.scalar_tensor_tensor(out=kk[:], in0=k[:], scalar=col("k_k_2"), in1=kk[:], op0=ALU.mult,
                                           op1=ALU.mult).then_inc(kk_done, 1)
            for d in range(2):
                dve.wait_ge(a_done, d + 1)
                nc.vector.tensor_scalar(src[:, d, 2], a[d][:], col("k_a_2"), core.one_ka[:, bass.ds(pr, 1)],
                                        ALU.mult, ALU.add).then_inc(kd_half, 1)
                dve.wait_ge(kd_half, d + 1)
                nc.vector.tensor_tensor(src[:, d, 2], src[:, d, 2], k[:], ALU.mult).then_inc(kd_done, 1)
            dve.wait_ge(kd_done, 2)
            nc.vector.tensor_tensor(t1[:], src[:, 0, 2], src[:, 1, 2], ALU.add).then_inc(sum_kd, 1)
            dve.wait_ge(sum_kd, 1)
            nc.vector.scalar_tensor_tensor(out=t1[:], in0=t1[:], scalar=col("r_k_2"), in1=r[:], op0=ALU.mult,
                                           op1=ALU.mult).then_inc(dots_in, 1)
            for d in range(2):
                dve.wait_ge(bar_exp, d + 1)
                dve.wait_ge(kk_done, 1)
                nc.vector.tensor_tensor(src[:, d, 0], kk[:], e[:], ALU.mult).then_inc(bar_used, 1)
                dve.wait_ge(p_exp, d + 1)
                end = CH - 1 if d == 0 else 0
                nc.vector.tensor_copy(pl[:, d], src[:, d, 1].rearrange("p (c t) -> p c t", t=CH)[:, :, end]
                                      ).then_inc(pl_done, 1)
                dve.wait_ge(pl_done, d + 1)
                nc.vector.tensor_tensor(src[:, d, 1], src[:, d, 1], r[:], ALU.mult).then_inc(p_used, 1)
                dve.wait_ge(m_exp, d + 1)
                dve.wait_ge(akk_done, d + 1)
                nc.vector.tensor_tensor(src[:, d, 2:4], src[:, d, 2:4], e.ap().unsqueeze(1).to_broadcast([P, 2, T]),
                                        ALU.mult).then_inc(m_used, 1)
                if d == 0:
                    dve.wait_ge(dots_mm, 1)
                    nc.vector.tensor_tensor(bonus[:], bank2(0), vc[:], ALU.mult).then_inc(bonus_done, 1)


class Step:

    def __init__(self, m, base):
        self.m, self.base, self.half = m, base, base % 2

    def v(self, per, plus=0):
        if self.m is None:
            return self.base * per + plus
        return self.m * (2 * per) + (self.base * per + plus)

    def tile(self, d):
        if d == 0:
            return self.v(1)
        return (TT - 1 - self.base) if self.m is None else self.m * -2 + (TT - 1 - self.base)

    def back(self, n):
        return None if self.m is None and self.base < n else Step(self.m, self.base - n)


def chunk_steps(eng, front, both, last):
    front(Step(None, 0))
    both(Step(None, 1))
    with eng.Fori(0, TT // 2 - 1) as m:
        both(Step(m, 2))
        both(Step(m, 3))
    last(Step(None, TT - 1))


def stage_rwkv_chunks(core):
    nc, ps, src = core.nc, core.psum, core.src
    yd = core.yd = [core.at(f"pair_out{d}", 28 + 4 * d, [P, TT, P]) for d in range(2)]
    vt = core.at("v_pair_tm", 36, [P, TT, P])
    khT = core.at("hats_turned", 40, [P, 2, 2, 2, P])
    am = core.at("masked_products", 44, [P, 2, 2, 2, 4, P])
    xs = core.at("operands_staged", 60, [P, 2, 2, 4, P])
    tt = core.at("inverse", 68, [P, 2, 2, 4, P])
    ym = core.at("inverse_step", 190, [P, 2, 2, P])
    kh = core.at("hats", 192, [P, 2, 2, P])
    vs = core.at("v_staged", 194, [P, 2, 2, P])
    rhs = core.at("u_rhs", 196, [P, 2, 2, RN])
    nu = core.at("minus_u", 197, [P, 2, 2, RN])
    z = core.at("pair_state", 198, [P, 2, RN])
    pl = core.pl2
    MKK, ARK, MKB, ARB = range(4)
    L = LEVELS - 1
    with Stage(core, "chunks") as s:
        (vt_mm, vt_out, z_zero, xs_staged, vs_staged, am_mm, am_done, kh_done, kh_mm, khT_done, mkb_mm, t_part,
         t_done, iy_mm, iy_done, it_mm, rhs_mm, rhs_done, u_mm, u_done, y_mm, y_out, z_mm, z_done) = s.sems(
            "vt_mm", "vt_out", "z_zero", "xs_staged", "vs_staged", "am_mm", "am_done", "kh_done", "kh_mm",
            "khT_done", "mkb_mm", "t_part", "t_done", "iy_mm", "iy_done", "it_mm", "rhs_mm", "rhs_done", "u_mm",
            "u_done", "y_mm", "y_out", "z_mm", "z_done")

        @s.b.gpsimd
        def _(pool):
            def front(n):
                two = n.back(2)
                if two is not None:
                    pool.wait_ge(y_mm, two.v(1, 1))
                for d in range(2):
                    ins = nc.gpsimd.tensor_copy(xs[:, n.half, d], src[:, d, :, bass.ds(n.tile(d) * P, P)])
                ins.then_inc(xs_staged, 1)
                if two is not None:
                    pool.wait_ge(z_mm, two.v(1, 1))
                for d in range(2):
                    ins = nc.gpsimd.tensor_copy(vs[:, n.half, d:d + 1], vt[:, bass.ds(n.tile(d), 1), :])
                ins.then_inc(vs_staged, 1)
            pool.wait_ge(vt_out, 1)
            chunk_steps(pool, front, front, lambda n: None)

        @s.b.tensor
        def _(pe):
            for t in range(TT):
                ins = nc.tensor.transpose(ps[:, t // 4, (t % 4) * P:(t % 4 + 1) * P], core.vc[:, t * P:(t + 1) * P],
                                          core.mask(M_ID))
            ins.then_inc(vt_mm, 1)
            pe.wait_ge(vt_out, 1)
            pe.wait_ge(z_zero, 1)

            def products(n):
                one = n.back(1)
                pe.wait_ge(xs_staged, n.v(1, 1))
                for d in range(2):
                    if one is not None or d:
                        pe.wait_ge(am_done, n.v(2, d))
                    for h in range(2):
                        a = slice(64 * h, 64 * h + 64)
                        right = xs[a, n.half, d, 0:2].rearrange("p k t -> p (k t)")
                        nc.tensor.matmul(ps[:, h, 0:256], xs[a, n.half, d, 2], right, start=True, stop=True)
                        ins = nc.tensor.matmul(ps[:, h, 256:512], xs[a, n.half, d, 3], right, start=True, stop=True)
                    ins.then_inc(am_mm, 1)
                pe.wait_ge(kh_done, n.v(1, 1))
                for d in range(2):
                    if one is not None:
                        pe.wait_ge(iy_done, n.v(2 * L, d - 1))
                    for m in range(2):
                        ins = nc.tensor.transpose(ps[:, 4 + d, 256 + P * m:256 + P * m + P], kh[:, d, m],
                                                  core.mask(M_ID))
                    ins.then_inc(kh_mm, 1)
                for d in range(2):
                    pe.wait_ge(am_done, n.v(2, d + 1))
                    if one is not None:
                        pe.wait_ge(t_done, n.v(2 * L + 2, d - 1))
                    for h in range(2):
                        ins = nc.tensor.transpose(ps[:, 6 + d, P * h:P * h + P], am[:, n.half, d, h, MKB],
                                                  core.mask(M_ID))
                    ins.then_inc(mkb_mm, 1)

            def level(n, l):
                for d in range(2):
                    pe.wait_ge(t_done, n.v(2 * L + 2, 2 * l + d - 1))
                    if l == 1:
                        pe.wait_ge(khT_done, n.v(2, d + 1))
                    for h in range(2):
                        ins = nc.tensor.matmul(ps[:, 4 + d, P * h:P * h + P], am[:, n.half, d, h, MKB],
                                               tt[:, n.half, d, h], start=True, stop=True)
                    ins.then_inc(iy_mm, 1)
                for d in range(2):
                    pe.wait_ge(iy_done, n.v(2 * L, 2 * l + d - 1))
                    for h in range(2):
                        if l < L:
                            nc.tensor.matmul(ps[:, 6 + d, P * h:P * h + P], tt[:, n.half, d, 2 + h], ym[:, d, h],
                                             start=True, stop=True)
                        ins = nc.tensor.matmul(ps[:, 6 + d, 256 + P * h:256 + P * h + P], ym[:, d, h],
                                               tt[:, n.half, d, 2 + h], start=True, stop=True)
                    ins.then_inc(it_mm, 1)

            def right_side(n):
                one = n.back(1)
                if one is not None:
                    pe.wait_ge(z_done, n.v(1))
                    pe.wait_ge(y_out, n.v(1))
                pe.wait_ge(vs_staged, n.v(1, 1))
                for d in range(2):
                    for h in range(2):
                        a = slice(64 * h, 64 * h + 64)
                        out = ps[:, 2 + h, RN * d:RN * d + RN]
                        nc.tensor.matmul(out, xs[a, n.half, d, 0], z[a, d], start=True, stop=False)
                        ins = nc.tensor.matmul(out, am[:, n.half, d, h, MKK], vs[:, n.half, d, a], start=False, stop=True)
                ins.then_inc(rhs_mm, 1)

            def solve(n):
                pe.wait_ge(rhs_done, n.v(1, 1))
                pe.wait_ge(t_done, n.v(2 * L + 2, 2 * L + 2))
                for d in range(2):
                    for h in range(2):
                        at = 256 + RN * (2 * d + h)
                        ins = nc.tensor.matmul(ps[:, 2, at:at + RN], tt[:, n.half, d, 2 + h], rhs[:, h, d],
                                               start=True, stop=True)
                ins.then_inc(u_mm, 1)

            def outputs(n):
                pe.wait_ge(u_done, n.v(1, 1))
                for d in range(2):
                    for h in range(2):
                        a = slice(64 * h, 64 * h + 64)
                        out = ps[:, 2 + h, P + RN * d:P + RN * d + RN]
                        nc.tensor.matmul(out, xs[a, n.half, d, 1], z[a, d], start=True, stop=False)
                        nc.tensor.matmul(out, am[:, n.half, d, h, ARK], vs[:, n.half, d, a], start=False, stop=False)
                        ins = nc.tensor.matmul(out, am[:, n.half, d, h, ARB], nu[:, d, h], start=False, stop=True)
                ins.then_inc(y_mm, 1)
                for d in range(2):
                    for h in range(2):
                        a = slice(64 * h, 64 * h + 64)
                        out = ps[a, 3, 256 + RN * d:256 + RN * d + RN]
                        nc.tensor.matmul(out, khT[:, n.half, d, 0, a], vs[:, n.half, d, a], start=True, stop=False)
                        ins = nc.tensor.matmul(out, khT[:, n.half, d, 1, a], nu[:, d, h], start=False, stop=True)
                ins.then_inc(z_mm, 1)

            def front(n):
                products(n)
                for l in range(1, L + 1):
                    level(n, l)

            def both(n):
                one = n.back(1)
                products(n)
                right_side(one)
                level(n, 1)
                solve(one)
                level(n, 2)
                outputs(one)
                for l in range(3, L + 1):
                    level(n, l)

            def last(n):
                right_side(n)
                solve(n)
                outputs(n)
            chunk_steps(pe, front, both, last)

        @s.b.scalar
        def _(act):
            act.wait_ge(vt_mm, 1)
            nc.scalar.activation(vt.ap().rearrange("p t n -> p (t n)"), ps[:, 0:2, :].rearrange("p b n -> p (b n)"),
                                 ACT.Copy).then_inc(vt_out, 1)

            def front(n):
                one = n.back(1)
                if one is not None:
                    act.wait_ge(kh_mm, n.v(2))
                for d in range(2):
                    ins = nc.scalar.activation(kh[:, d], src[:, d, 2:4, bass.ds(n.tile(d) * P, P)], ACT.Copy,
                                               scale=pl[:, d, bass.ds(n.tile(d), 1)])
                ins.then_inc(kh_done, 1)
                two = n.back(2)
                for d in range(2):
                    act.wait_ge(kh_mm, n.v(2, d + 1))
                    if two is not None and d == 0:
                        act.wait_ge(z_mm, two.v(1, 1))
                    nc.scalar.activation(khT[:, n.half, d], ps[:, 4 + d, 256:512].rearrange("p (m t) -> p m t", m=2),
                                         ACT.Copy).then_inc(khT_done, 1)

            def back(n):
                one = n.back(1)
                act.wait_ge(rhs_mm, n.v(1, 1))
                if one is not None:
                    act.wait_ge(u_mm, n.v(1))
                nc.scalar.activation(rhs[:], ps[:, 2:4, 0:P].rearrange("p h (d n) -> p h d n", d=2), ACT.Copy
                                     ).then_inc(rhs_done, 1)
                act.wait_ge(u_mm, n.v(1, 1))
                if one is not None:
                    act.wait_ge(z_mm, n.v(1))
                nc.scalar.activation(nu[:], ps[:, 2, 256:512].rearrange("p (d h n) -> p d h n", d=2, h=2), ACT.Copy,
                                     scale=-1.0).then_inc(u_done, 1)
                act.wait_ge(z_mm, n.v(1, 1))
                for d in range(2):
                    out = yd[d][:, bass.ds(n.tile(d), 1), :].rearrange("p a (h n) -> p (a h) n", h=2)
                    ins = nc.scalar.activation(out, ps[:, 2:4, P + RN * d:P + RN * d + RN], ACT.Copy)
                ins.then_inc(y_out, 1)

            def both(n):
                front(n)
                back(n.back(1))
            chunk_steps(act, front, both, back)

        @s.b.vector
        def _(dve):
            nc.vector.memset(z[:], 0.0).then_inc(z_zero, 1)

            def start(n):
                one, two = n.back(1), n.back(2)
                for d in range(2):
                    dve.wait_ge(am_mm, n.v(2, d + 1))
                    if two is not None and d == 0:
                        dve.wait_ge(y_mm, two.v(1, 1))
                    nc.vector.tensor_tensor(am[:, n.half, d].rearrange("p h k t -> p h (k t)"), ps[:, 0:2, :],
                                            core.mask4[:, d:d + 1].rearrange("p a k t -> p a (k t)").to_broadcast(
                                                [P, 2, 512]), ALU.mult).then_inc(am_done, 1)
                for d in range(2):
                    low = (M_LO, M_UP)
                    dve.wait_ge(am_done, n.v(2, d + 1))
                    nc.vector.scalar_tensor_tensor(
                        out=tt[:, n.half, d, 2:4], in0=am[:, n.half, d, :, MKB], scalar=-1.0,
                        in1=core.masks[:, low[1 - d]:low[1 - d] + 1, :].to_broadcast([P, 2, P]),
                        op0=ALU.mult, op1=ALU.mult)
                    dve.wait_ge(mkb_mm, n.v(2, d + 1))
                    nc.vector.scalar_tensor_tensor(
                        out=tt[:, n.half, d, 0:2], in0=ps[:, 6 + d, 0:256].rearrange("p (h t) -> p h t", h=2),
                        scalar=-1.0, in1=core.masks[:, low[d]:low[d] + 1, :].to_broadcast([P, 2, P]),
                        op0=ALU.mult, op1=ALU.mult).then_inc(t_part, 1)
                    dve.wait_ge(t_part, n.v(2, d + 1))
                    nc.vector.tensor_tensor(tt[:, n.half, d], tt[:, n.half, d],
                                            core.masks[:, M_ID:M_ID + 1, :].to_broadcast([P, 4, P]), ALU.add
                                            ).then_inc(t_done, 1)

            def level(n, l):
                for d in range(2):
                    m = (M_LO, M_UP)[d] + l
                    dve.wait_ge(iy_mm, n.v(2 * L, 2 * l + d - 1))
                    if l > 1 or n.back(1) is not None:
                        dve.wait_ge(it_mm, n.v(2 * L, 2 * l + d - 3))
                    nc.vector.tensor_tensor(ym[:, d], ps[:, 4 + d, 0:256].rearrange("p (h t) -> p h t", h=2),
                                            core.masks[:, m:m + 1, :].to_broadcast([P, 2, P]), ALU.mult
                                            ).then_inc(iy_done, 1)
                for d in range(2):
                    dve.wait_ge(it_mm, n.v(2 * L, 2 * l + d - 1))
                    dve.wait_ge(t_done, n.v(2 * L + 2, 2 * l + d - 1))
                    a = slice(0, 4) if l < L else slice(2, 4)
                    nc.vector.tensor_tensor(tt[:, n.half, d, a], tt[:, n.half, d, a],
                                            ps[:, 6 + d, a.start * P:512].rearrange("p (k t) -> p k t", t=P),
                                            ALU.subtract).then_inc(t_done, 1)

            def state(n):
                dve.wait_ge(z_mm, n.v(1, 1))
                if n.back(1) is not None:
                    dve.wait_ge(z_done, n.v(1))
                dve.wait_ge(y_out, n.v(1, 1))
                for d in range(2):
                    ins = nc.vector.scalar_tensor_tensor(out=z[:, d], in0=z[:, d], scalar=pl[:, d, bass.ds(n.tile(d), 1)],
                                                         in1=ps[:, 3, 256 + RN * d:256 + RN * d + RN],
                                                         op0=ALU.mult, op1=ALU.add)
                ins.then_inc(z_done, 1)

            def front(n):
                start(n)
                for l in range(1, L + 1):
                    level(n, l)

            def both(n):
                start(n)
                level(n, 1)
                level(n, 2)
                level(n, 3)
                state(n.back(1))
                for l in range(4, L + 1):
                    level(n, l)
            dve.wait_ge(z_zero, 1)
            chunk_steps(dve, front, both, state)


def stage_rwkv_out(core, pr):
    nc, dram, ps = core.nc, core.dram, core.psum
    flat = ps.ap().rearrange("p b n -> p (b n)")
    yf, yb = core.yd
    G = 2 * TT
    sq = core.at("pair_squares", 44, [P, TT, P])
    cm = core.at("pair_out_cm", 48, [P, T])
    gup = core.at("w_g_up", 52, [P, P])
    stat = core.at("group_stat", 53, [P, 4, G])
    col = lambda name: core.pcol[:, bass.ds(pr + PCOL[name], 1)]
    by_head = lambda a: a.ap().rearrange("p t (h n) -> p (t h) n", n=RN)
    with Stage(core, "pair_out") as s:
        gup_in, g_mm, summed, squared, order, rooted, centred, scaled, turned, cm_out, with_bonus, done = s.sems(
            "gup_in", "g_mm", "summed", "squared", "order", "rooted", "centred", "scaled", "turned", "cm_out",
            "with_bonus", "done")

        @s.b.sync
        def _(sp):
            sp.dma_start(gup[:], dram["g_up_2"][0][:, bass.ds(pr * P, P)]).then_inc(gup_in, 16)

        @s.b.vector
        def _(dve):
            nc.vector.tensor_tensor(yf[:], yf[:], yb[:], ALU.add).then_inc(summed, 1)
            dve.wait_ge(summed, 1)
            nc.vector.reduce_sum(stat[:, 0], by_head(yf), axis=AX).then_inc(order, 1)
            dve.wait_ge(order, 1)
            nc.vector.tensor_scalar(stat[:, 0], stat[:, 0], 1.0 / RN, None, ALU.mult).then_inc(order, 1)
            dve.wait_ge(order, 2)
            nc.vector.tensor_tensor(by_head(yf), by_head(yf), stat[:, 0].unsqueeze(2).to_broadcast([P, G, RN]),
                                    ALU.subtract).then_inc(centred, 1)
            dve.wait_ge(squared, 1)
            nc.vector.reduce_sum(stat[:, 1], by_head(sq), axis=AX).then_inc(order, 1)
            dve.wait_ge(order, 3)
            nc.vector.tensor_scalar(stat[:, 1], stat[:, 1], 1.0 / RN, LNX_EPS, ALU.mult, ALU.add).then_inc(order, 1)
            dve.wait_ge(rooted, 1)
            nc.vector.reciprocal(stat[:, 3], stat[:, 2]).then_inc(order, 1)
            dve.wait_ge(order, 5)
            nc.vector.tensor_tensor(by_head(yf), by_head(yf), stat[:, 3].unsqueeze(2).to_broadcast([P, G, RN]),
                                    ALU.mult).then_inc(scaled, 1)
            dve.wait_ge(cm_out, 1)
            nc.vector.tensor_tensor(cm[:], cm[:], core.bonus[:], ALU.add).then_inc(with_bonus, 1)
            dve.wait_ge(with_bonus, 1)
            dve.wait_ge(g_mm, 1)
            nc.vector.tensor_tensor(core.yrT[:, bass.ds(pr, 1), :].rearrange("p a t -> p (a t)"), cm[:],
                                    flat[:, 1024:1024 + T], ALU.mult).then_inc(done, 1)

        @s.b.scalar
        def _(act):
            nc.scalar.preload_act_table(ACT.Sqrt)
            act.wait_ge(centred, 1)
            nc.scalar.activation(sq[:], yf[:], ACT.Square).then_inc(squared, 1)
            act.wait_ge(order, 4)
            nc.scalar.activation(stat[:, 2], stat[:, 1], ACT.Sqrt).then_inc(rooted, 1)
            act.wait_ge(turned, 1)
            nc.scalar.activation(cm[:], flat[:, 0:T], ACT.Identity, bias=col("ln_x_b_2"), scale=col("ln_x_w_2")
                                 ).then_inc(cm_out, 1)

        @s.b.tensor
        def _(pe):
            pe.wait_ge(gup_in, 16)
            for h in range(2):
                ins = nc.tensor.matmul(ps[:, 2 + h, :], gup[:], core.lows[:, 0, 512 * h:512 * h + 512],
                                       start=True, stop=True)
            ins.then_inc(g_mm, 1)
            pe.wait_ge(scaled, 1)
            for t in range(TT):
                ins = nc.tensor.transpose(ps[:, t // 4, (t % 4) * P:(t % 4 + 1) * P], yf[:, t], core.mask(M_ID))
            ins.then_inc(turned, 1)


def rwkv_pairs(core, hT):
    with core.nc.Fori(0, RH // 2) as pr:
        stage_rwkv_prepare(core, hT, pr)
        stage_rwkv_chunks(core)
        stage_rwkv_out(core, pr)


ROW_MIX, ROW_FFN, ROW_FINAL = 12, 28, 32


def stage_merge(core, hT):
    nc, dram, ps = core.nc, core.dram, core.psum
    mt = core.merged = core.at("merged_cm", 124, [P, KD, T])
    hT_split = (core.at("mixers_high", 44, [P, KD, T], F32R), core.at("mixers_low", 76, [P, KD, T], F32R))
    wg = core.at("w_gates_raw", 156, [P, 2, KD, P])
    wg_split = core.at("w_gates_split", 164, [P, 2, 2, 2, KD, P], F32R)
    wp = core.at("w_projections", 36, [P, 2, 2, 4, P])
    sg = core.at("gates_sb", 196, [P, 2, 2, 512])
    core.g_ffn = core.at("gain_ffn", ROW_FFN, [P, D])
    core.g_final = core.at("gain_final", ROW_FINAL, [P, D])
    mixers = (core.yrT, core.yaT)
    with Stage(core, "merge") as s:
        wp_in = [s.sem(f"wp_in{j}") for j in range(2)]
        passed_sp = s.sem("passed_sp")
        wg_in, row_in, h_high, h_low, high, low, g_mm, p_mm, g_out, parts, order = s.sems(
            "wg_in", "row_in", "h_high", "h_low", "high", "low", "g_mm", "p_mm", "g_out", "parts", "order")

        @s.b.sync
        def _(sp):
            def load(i, before):
                for j in range(2):
                    if before is not None or j:
                        sp.wait_ge(low, i * 2 + j)
                        passed(sp, passed_sp)
                    for g, first in enumerate((C2_GR, C2_GA)):
                        sp.dma_start(wg[:, g], weight_columns(dram["w_in_2"][0], i * 256 + first + P * j, P)
                                     ).then_inc(wg_in, 16)
                    if before is not None:
                        sp.wait_ge(p_mm, before * 4 + (2 * j + 2))
                        passed(sp, passed_sp)
                    for g, name in enumerate(("w_proj_rwkv_2", "w_proj_attn_2")):
                        sp.dma_start(wp[:, j, g], weight_columns(dram[name][0], i * 256 + P * j, P)
                                     ).then_inc(wp_in[j], 16)
            run_loop(sp, KD // 2, load)

        @s.b.tensor
        def _(pe):
            pe.wait_ge(h_low, 2)

            def work(i, before):
                for j in range(2):
                    for h in range(2):
                        cols = slice(512 * h, 512 * h + 512)
                        if before is not None or j:
                            pe.wait_ge(order, i * 4 + (2 * j + h - 1))
                        if h == 0:
                            pe.wait_ge(low, i * 2 + (j + 1))
                        for g in range(2):
                            for k in range(KD):
                                ins = split_product(nc, ps[:, 4 * h + g, :], [wg_split[:, j, g, m, k] for m in range(2)],
                                                    [a[:, k, cols] for a in hT_split], k == 0, k == KD - 1)
                        ins.then_inc(g_mm, 1)
                        if h == 0:
                            pe.wait_ge(wp_in[j], i * 32 + 32)
                        for g in range(2):
                            for k in range(4):
                                ins = nc.tensor.matmul(ps[:, 4 * h + 2 + g, :], wp[:, j, g, k], mixers[g][:, k, cols],
                                                       start=(k == 0), stop=(k == 3))
                        ins.then_inc(p_mm, 1)
            run_loop(pe, KD // 2, work)

        @s.b.scalar
        def _(act):
            nc.scalar.preload_act_table(ACT.Sigmoid)
            act.dma_start(core.g_ffn[:], dram_row(dram["norm_ffn_g_2"], D)).then_inc(row_in, 16)
            act.dma_start(core.g_final[:], dram["norm_final_g_2"].rearrange("(a n) -> a n", a=1).to_broadcast([P, D])
                          ).then_inc(row_in, 16)
            for h in range(2):
                high_part(nc, hT_split[0][:, 4 * h:4 * h + 4], hT[:, 4 * h:4 * h + 4]).then_inc(h_high, 1)

            def split(i, before, j):
                act.wait_ge(wg_in, i * 64 + (32 * j + 32))
                if before is not None:
                    act.wait_ge(g_mm, before * 4 + (2 * j + 2))
                high_part(nc, wg_split[:, j, :, 0], wg[:]).then_inc(high, 1)

            def gates(i, j):
                for h in range(2):
                    n = 2 * (j - 1) + h
                    act.wait_ge(g_mm, i * 4 + (n + 1))
                    if not (isinstance(i, int) and i == 0 and j == 1):
                        act.wait_ge(order, i * 4 + (n - 1))
                    nc.scalar.activation(sg[:, h], ps[:, 4 * h:4 * h + 2, :], ACT.Sigmoid).then_inc(g_out, 1)

            def work(i, before):
                for j in range(2):
                    split(i, before, j)
                    if before is not None or j:
                        gates(i, j)
            run_loop(act, KD // 2, work)
            gates(KD // 2, 0)
            act.wait_ge(row_in, 32)

        @s.b.vector
        def _(dve):
            for h in range(2):
                dve.wait_ge(h_high, h + 1)
                low_part(nc, hT_split[1][:, 4 * h:4 * h + 4], hT[:, 4 * h:4 * h + 4],
                         hT_split[0][:, 4 * h:4 * h + 4]).then_inc(h_low, 1)

            def merged(i, j):
                for h in range(2):
                    n = 2 * (j - 1) + h
                    dve.wait_ge(g_out, i * 4 + (n + 1))
                    dve.wait_ge(p_mm, i * 4 + (n + 1))
                    nc.vector.tensor_tensor(sg[:, h], sg[:, h], ps[:, 4 * h + 2:4 * h + 4, :], ALU.mult
                                            ).then_inc(parts, 1)
                    dve.wait_ge(parts, i * 4 + (n + 1))
                    nc.vector.tensor_tensor(mt[:, bass.ds(i * 2 + (j - 1), 1), 512 * h:512 * h + 512].rearrange(
                        "p a t -> p (a t)"), sg[:, h, 0], sg[:, h, 1], ALU.add).then_inc(order, 1)

            def work(i, before):
                for j in range(2):
                    dve.wait_ge(high, i * 2 + (j + 1))
                    low_part(nc, wg_split[:, j, :, 1], wg[:], wg_split[:, j, :, 0]).then_inc(low, 1)
                    if before is not None or j:
                        merged(i, j)
            run_loop(dve, KD // 2, work)
            merged(KD // 2, 0)


def stage_router(core, hT):
    nc, dram, ps = core.nc, core.dram, core.psum
    wr = core.at("w_router", 12, [P, KD, NE])
    aff = core.at("affinity", 13, [P, TT, NE])
    stat = core.at("router_stat", 14, [P, 3, TT])
    affT = core.at("affinity_turned", 108, [NE, 2, T])
    top = core.at("top_values", 116, [NE, CAP])
    topi = core.at("top_tokens", 117, [NE, CAP], U32)
    topf = core.at("top_tokens_f", 118, [NE, CAP])
    core.vals = core.at("expert_values", 15, [P, NE])
    core.idx = core.at("expert_tokens", 15.25, [P, NE], U32)
    with Stage(core, "router") as s:
        w_in, x_out, mm, order, exp_done, aff_done, turned, affT_done, found, placed, cut, number, back_mm, done = s.sems(
            "w_in", "x_out", "mm", "order", "exp_done", "aff_done", "turned", "affT_done", "found", "placed", "cut",
            "number", "back_mm", "done")

        @s.b.sync
        def _(sp):
            sp.dma_start(wr[:], dram["w_router_2"][0].rearrange("(k p) n -> p k n", p=P)).then_inc(w_in, 16)
            sp.dma_start(dram["stream"].rearrange("(t p) d -> p t d", p=P), core.x[:]).then_inc(x_out, 16)
            sp.wait_ge(x_out, 16)

        @s.b.tensor
        def _(pe):
            pe.wait_ge(w_in, 16)
            for t in range(TT):
                for k in range(KD):
                    ins = nc.tensor.matmul(ps[:, 0, t * NE:(t + 1) * NE], hT[:, k, t * P:(t + 1) * P], wr[:, k],
                                           start=(k == 0), stop=(k == KD - 1))
            ins.then_inc(mm, 1)
            pe.wait_ge(aff_done, 1)
            for t in range(TT):
                ins = nc.tensor.transpose(ps[0:NE, 1 + t // 4, (t % 4) * P:(t % 4 + 1) * P], aff[:, t], core.mask(M_ID))
            ins.then_inc(turned, 1)
            pe.wait_ge(number, 1)
            nc.tensor.transpose(ps[:, 3, 0:NE], top[:], core.masks[0:NE, M_ID, 0:NE])
            nc.tensor.transpose(ps[:, 3, NE:2 * NE], topf[:], core.masks[0:NE, M_ID, 0:NE]).then_inc(back_mm, 1)

        @s.b.scalar
        def _(act):
            act.wait_ge(order, 2)
            nc.scalar.activation(aff[:], aff[:], ACT.Exp).then_inc(exp_done, 1)

        @s.b.vector
        def _(dve):
            logits = ps[:, 0, 0:TT * NE].rearrange("p (t e) -> p t e", e=NE)
            over = lambda n: stat[:, n].unsqueeze(2).to_broadcast([P, TT, NE])
            dve.wait_ge(mm, 1)
            nc.vector.reduce_max(stat[:, 0], logits, axis=AX).then_inc(order, 1)
            dve.wait_ge(order, 1)
            nc.vector.tensor_tensor(aff[:], logits, over(0), ALU.subtract).then_inc(order, 1)
            dve.wait_ge(exp_done, 1)
            nc.vector.reduce_sum(stat[:, 1], aff[:], axis=AX).then_inc(order, 1)
            dve.wait_ge(order, 3)
            nc.vector.reciprocal(stat[:, 2], stat[:, 1]).then_inc(order, 1)
            dve.wait_ge(order, 4)
            nc.vector.tensor_tensor(aff[:], aff[:], over(2), ALU.mult).then_inc(aff_done, 1)
            dve.wait_ge(turned, 1)
            nc.vector.tensor_copy(affT[:, 0], ps[0:NE, 1:3, :].rearrange("p b n -> p (b n)")).then_inc(affT_done, 1)
            dve.wait_ge(affT_done, 1)
            for r in range(CAP // 8):
                a = slice(8 * r, 8 * r + 8)
                now, then = affT[:, r % 2], affT[:, (r + 1) % 2]
                if r:
                    dve.wait_ge(cut, r)
                nc.vector.max(top[:, a], now).then_inc(found, 1)
                dve.wait_ge(found, r + 1)
                nc.vector.max_index(topi[:, a], top[:, a], now).then_inc(placed, 1)
                nc.vector.match_replace(then, top[:, a], now, -1.0).then_inc(cut, 1)
            dve.wait_ge(placed, CAP // 8)
            nc.vector.tensor_copy(topf[:], topi[:]).then_inc(number, 1)
            dve.wait_ge(back_mm, 1)
            nc.vector.tensor_copy(core.vals[:], ps[:, 3, 0:NE]).then_inc(done, 1)
            nc.vector.tensor_copy(core.idx[:], ps[:, 3, NE:2 * NE]).then_inc(done, 1)


def stage_experts(core):
    nc, dram, ps = core.nc, core.dram, core.psum
    H = EF // 2
    wt = [core.at(f"w_exp{n}", 76 + 16 * n, [P, KD, H]) for n in range(6)]
    xg = core.at("x_gathered", 44, [P, 2, D])
    xT = core.at("x_turned", 52, [P, 2, KD, P])
    hid = core.at("expert_hidden", 60, [P, EF])
    hT = core.at("hidden_turned", 64, [P, KD, P])
    sil = core.at("silu_gate", 68, [P, 2, H])
    ys = core.at("expert_out", 172, [P, 2, D])
    idx = core.at("token_column", 16, [P, 2, 8], U32)
    with Stage(core, "experts") as s:
        w_in = [s.sem(f"w_in{n}") for n in range(6)]
        x_in = [s.sem(f"x_in{j}") for j in range(2)]
        idx_done, x_turned, xT_done, gu_mm, silu_done, hid_done, h_turned, hT_done, w_used, ys_done, y_mm, added = s.sems(
            "idx_done", "x_turned", "xT_done", "gu_mm", "silu_done", "hid_done", "h_turned", "hT_done", "w_used",
            "ys_done", "y_mm", "added")
        passed_sp, passed_pool = s.sems("passed_sp", "passed_pool")
        names = ("gate", "up", "gate", "up", "down", "down")

        def experts(eng, body):
            body(0, None, False)
            with eng.Fori(0, NE // 2 - 2) as before:
                body(before + 1, before, False)
            body(NE // 2 - 1, NE // 2 - 2, True)

        @s.b.sync
        def _(sp):
            def load(i, before, last):
                for j in range(2):
                    for n, name in enumerate(names):
                        if before is not None or j:
                            sp.wait_ge(w_used, i * 12 + (6 * j + n - 5))
                            passed(sp, passed_sp)
                        half = n // 2 if n < 4 else n - 4
                        src = dram[f"exp_w_{name}_2"][0][bass.ds(i * 2 + j, 1)].rearrange(
                            "a (k p) n -> p (a k) n", p=P)[:, :, H * half:H * half + H]
                        sp.dma_start(wt[n][:], src).then_inc(w_in[n], 16)
            experts(sp, load)

        @s.b.gpsimd
        def _(pool):
            def gather(e_expr, j, turned_wait, n_idx):
                if turned_wait is not None:
                    pool.wait_ge(x_turned, turned_wait)
                    passed(pool, passed_pool)
                nc.gpsimd.tensor_copy(idx[:, j, 0:1], core.idx[:, bass.ds(e_expr, 1)]).then_inc(idx_done, 1)
                pool.wait_ge(idx_done, n_idx)
                passed(pool, passed_pool)
                nc.gpsimd.indirect_dma_start(xg[:, j], None, dram["hidden"],
                                             bass.IndirectOffsetOnAxis(idx[:, j, 0:1], 0)).then_inc(x_in[j], 16)

            def work(i, before, last):
                for j in range(2):
                    if not (last and j):
                        gather(i * 2 + (j + 1), 1 - j, None if before is None and j == 0 else i * 2 + j,
                               i * 4 + (2 * j + 2))
                    if before is not None or j:
                        pool.wait_ge(added, i * 32 + 16 * j)
                        passed(pool, passed_pool)
                    nc.gpsimd.tensor_copy(idx[:, j, 1:2], core.idx[:, bass.ds(i * 2 + j, 1)]).then_inc(idx_done, 1)
                    pool.wait_ge(idx_done, i * 4 + (2 * j + (2 if last and j else 3)))
                    pool.wait_ge(ys_done, i * 2 + (j + 1))
                    passed(pool, passed_pool)
                    nc.gpsimd.indirect_dma_start(dram["stream"], bass.IndirectOffsetOnAxis(idx[:, j, 1:2], 0),
                                                 ys[:, j], None, compute_op=ALU.add).then_inc(added, 16)
            gather(0, 0, None, 1)
            experts(pool, work)
            pool.wait_ge(added, 16 * NE)

        @s.b.tensor
        def _(pe):
            def turn_x(j, in_wait, out_wait):
                pe.wait_ge(x_in[j], in_wait)
                if out_wait is not None:
                    pe.wait_ge(xT_done, out_wait)
                for k in range(KD):
                    ins = nc.tensor.transpose(ps[:, k // 4, (k % 4) * P:(k % 4 + 1) * P], xg[:, j, k * P:(k + 1) * P],
                                              core.mask(M_ID))
                ins.then_inc(x_turned, 1)

            def work(i, before, last):
                for j in range(2):
                    pe.wait_ge(xT_done, i * 2 + (j + 1))
                    for n in range(4):
                        pe.wait_ge(w_in[n], i * 32 + 16 * (j + 1))
                        if n % 2 == 0 and (before is not None or j):
                            pe.wait_ge(hT_done, i * 2 + j)
                            pe.wait_ge(hid_done, i * 4 + (2 * j + n // 2 - 1))
                        for k in range(KD):
                            ins = nc.tensor.matmul(ps[:, 2 + n, :], xT[:, j, k], wt[n][:, k],
                                                   start=(k == 0), stop=(k == KD - 1))
                        ins.then_inc(w_used, 1)
                    if not (last and j):
                        turn_x(1 - j, i * 16 + (16 if j == 0 else 32), i * 2 + (j + 1))
                    pe.wait_ge(hid_done, i * 4 + (2 * j + 2))
                    for k in range(KD):
                        ins = nc.tensor.transpose(ps[:, 2 + k // 4, (k % 4) * P:(k % 4 + 1) * P],
                                                  hid[:, k * P:(k + 1) * P], core.mask(M_ID))
                    ins.then_inc(h_turned, 1)
                    pe.wait_ge(hT_done, i * 2 + (j + 1))
                    if before is not None or j:
                        pe.wait_ge(ys_done, i * 2 + j)
                    for n in range(2):
                        pe.wait_ge(w_in[4 + n], i * 32 + 16 * (j + 1))
                        for k in range(KD):
                            ins = nc.tensor.matmul(ps[:, 6 + n, :], hT[:, k], wt[4 + n][:, k],
                                                   start=(k == 0), stop=(k == KD - 1))
                        ins.then_inc(w_used, 1)
            turn_x(0, 16, None)
            experts(pe, work)

        @s.b.scalar
        def _(act):
            nc.scalar.preload_act_table(ACT.Silu)

            def take_x(j, n):
                act.wait_ge(x_turned, n)
                nc.scalar.activation(xT[:, j].rearrange("p k t -> p (k t)"), ps[:, 0:2, :].rearrange("p b n -> p (b n)"),
                                     ACT.Copy).then_inc(xT_done, 1)

            def work(i, before, last):
                for j in range(2):
                    for f in range(2):
                        act.wait_ge(w_used, i * 12 + (6 * j + 2 * f + 2))
                        if before is not None or j:
                            act.wait_ge(hid_done, i * 4 + (2 * j + f - 1))
                        nc.scalar.activation(sil[:, f], ps[:, 2 + 2 * f, :], ACT.Silu).then_inc(silu_done, 1)
                    if not (last and j):
                        take_x(1 - j, i * 2 + (j + 2))
                    act.wait_ge(w_used, i * 12 + (6 * j + 6))
                    nc.scalar.activation(ys[:, j], ps[:, 6:8, :].rearrange("p b n -> p (b n)"), ACT.Copy,
                                         scale=core.vals[:, bass.ds(i * 2 + j, 1)]).then_inc(ys_done, 1)
            take_x(0, 1)
            experts(act, work)

        @s.b.vector
        def _(dve):
            def work(i, before, last):
                for j in range(2):
                    for f in range(2):
                        dve.wait_ge(silu_done, i * 4 + (2 * j + f + 1))
                        if (before is not None or j) and f == 0:
                            dve.wait_ge(h_turned, i * 2 + j)
                        nc.vector.tensor_tensor(hid[:, H * f:H * f + H], sil[:, f], ps[:, 3 + 2 * f, :], ALU.mult
                                                ).then_inc(hid_done, 1)
                    dve.wait_ge(h_turned, i * 2 + (j + 1))
                    if before is not None or j:
                        dve.wait_ge(w_used, i * 12 + 6 * j)
                    nc.vector.tensor_copy(hT.ap().rearrange("p k t -> p (k t)"),
                                          ps[:, 2:4, :].rearrange("p b n -> p (b n)")).then_inc(hT_done, 1)
            experts(dve, work)


def stage_final(core):
    nc, dram, x = core.nc, core.dram, core.x
    junk = core.at("final_junk", 76, [P, D])
    out = core.at("final_rows", 80, [P, 2, D])
    stat = core.at("final_stat", 10.25, [P, 3, TT])
    with Stage(core, "final") as s:
        x_in = [s.sem(f"x_in{t}") for t in range(TT)]
        squared, order, rooted, done = s.sems("squared", "order", "rooted", "done")
        stored = [s.sem(f"stored{j}") for j in range(2)]

        @s.b.sync
        def _(sp):
            for t in range(TT):
                sp.dma_start(x[:, t], dram["stream"][t * P:(t + 1) * P, :]).then_inc(x_in[t], 16)
            for t in range(TT):
                sp.wait_ge(done, t + 1)
                sp.dma_start(dram["out"][0][t * P:(t + 1) * P, :], out[:, t % 2]).then_inc(stored[t % 2], 16)
            for j in range(2):
                sp.wait_ge(stored[j], 16 * (TT // 2))

        @s.b.scalar
        def _(act):
            nc.scalar.preload_act_table(ACT.Sqrt)
            for t in range(TT):
                act.wait_ge(x_in[t], 16)
                if t:
                    act.wait_ge(squared, t)
                nc.scalar.activation(junk[:], x[:, t], ACT.Square, accum_out=stat[:, 0, t:t + 1]).then_inc(squared, 1)
                act.wait_ge(order, 2 * t + 1)
                nc.scalar.activation(stat[:, 2, t:t + 1], stat[:, 1, t:t + 1], ACT.Sqrt).then_inc(rooted, 1)

        @s.b.vector
        def _(dve):
            for t in range(TT):
                dve.wait_ge(squared, t + 1)
                nc.vector.tensor_scalar(stat[:, 1, t:t + 1], stat[:, 0, t:t + 1], 1.0 / D, EPS, ALU.mult, ALU.add
                                        ).then_inc(order, 1)
                dve.wait_ge(rooted, t + 1)
                nc.vector.reciprocal(stat[:, 0, t:t + 1], stat[:, 2, t:t + 1]).then_inc(order, 1)
                dve.wait_ge(order, 2 * t + 2)
                if t >= 2:
                    dve.wait_ge(stored[t % 2], 16 * (t // 2))
                nc.vector.scalar_tensor_tensor(out=out[:, t % 2], in0=x[:, t], scalar=stat[:, 0, t:t + 1],
                                               in1=core.g_final[:], op0=ALU.mult, op1=ALU.mult).then_inc(done, 1)


def second_block(core):
    dram = core.dram
    hT = core.at("mixers_hT", 76, [P, KD, T])
    core.g_mix = core.at("gain_mix", ROW_MIX, [P, D])
    stage_norm_turn(core, "norm3", [(core.x2, TT, core.g_mix[:], None, hT, 0)], 108,
                    load=((core.g_mix[:], dram_row(dram["norm_mix_g_2"], D)),))
    stage_attention_project(core, hT)
    stage_attention(core)
    stage_rwkv_low(core, hT)
    rwkv_pairs(core, hT)
    stage_merge(core, hT)
    stage_into_stream(core, "mix2_out", KD, lambda k, g: core.merged[:, k, g * 512:g * 512 + 512],
                      dram["w_out_2"][0], 76, 92, 108, 180, core.x, dram["stream"])
    hT = core.at("moe_hT", 76, [P, KD, T])
    stage_norm_turn(core, "norm4", [(core.x, TT, core.g_ffn[:], None, hT, 0)], 130, store=dram["hidden"])
    stage_router(core, hT)
    stage_experts(core)
    stage_final(core)


def kernel(**inputs):
    import numpy as _np
    import concourse.bacc as _bacc
    from concourse import mybir as _mybir
    from concourse.bass_utils import run_bass_kernel_spmd as _run

    nc = _bacc.Bacc("TRN2", target_bir_lowering=False, num_devices=1)
    arrays = {name: _np.ascontiguousarray(a) for name, a in inputs.items()}
    arrays["masks"] = mask_table()
    arrays["alibi"] = alibi_table()
    dram = {name: nc.dram_tensor(f"in_{name}", a.shape, _mybir.dt.from_np(a.dtype), kind="ExternalInput").ap()
            for name, a in arrays.items()}
    dram["stream"] = nc.dram_tensor("stream", (T, D), F32, kind="Internal").ap()
    dram["hidden"] = nc.dram_tensor("hidden", (T, D), F32, kind="Internal").ap()
    dram["out"] = nc.dram_tensor("out", (1, T, D), F32, kind="ExternalOutput").ap()
    core = Core(nc, dram)
    first_block(core)
    second_block(core)
    r = _run(nc, [{f"in_{name}": a for name, a in arrays.items()}], core_ids=[0])
    return r.results[0]["out"]
```
